# Optimizing a Trainium2 kernel written in Bass

```python
import math
import jax, jax.numpy as jnp
from jax import lax
import numpy as np

D_MODEL = 1024
BATCH = 1
SEQ = 512
DEPTH = 2

HEAD_DIM = 64
N_HEADS = D_MODEL // HEAD_DIM
N_FOX = N_HEADS // 2
N_SB = N_HEADS - N_FOX
FOX_W = N_FOX * HEAD_DIM
SB_W = N_SB * HEAD_DIM
EVEN_IN = 3 * FOX_W + 3 * SB_W + N_FOX
N_Q = N_HEADS
N_KV = 4
GROUP = N_Q // N_KV
ODD_IN = N_Q * HEAD_DIM + 2 * N_KV * HEAD_DIM
WINDOW = 128
BLOCK_Q = 128
ROPE_THETA = 10000.0
D_FF = ((8 * D_MODEL // 3 + 255) // 256) * 256
PLE_DIM = 256
N_EVEN = (DEPTH + 1) // 2
N_ODD = DEPTH // 2
EPS = 1e-6
NEG_INF = -1e30

kernel_name = "hybrid_fox_stickbreak_swa_sink_block"

def _rmsnorm(x, g):
    xf = x.astype(jnp.float32)
    y = xf * lax.rsqrt(jnp.mean(xf * xf, axis=-1, keepdims=True) + EPS)
    return (y * g.astype(jnp.float32)).astype(x.dtype)

def _rope(x, pos):
    half = x.shape[-1] // 2
    inv = ROPE_THETA ** (-jnp.arange(half, dtype=jnp.float32) / half)
    ang = pos.astype(jnp.float32)[..., None] * inv
    cos = jnp.cos(ang)[:, :, None, :]
    sin = jnp.sin(ang)[:, :, None, :]
    xf = x.astype(jnp.float32)
    x1, x2 = xf[..., :half], xf[..., half:]
    out = jnp.concatenate([x1 * cos - x2 * sin, x2 * cos + x1 * sin], axis=-1)
    return out.astype(x.dtype)

def _forgetting_attention(q, k, v, log_f):
    S, d = q.shape[1], q.shape[-1]
    scale = d ** -0.5
    cum = jnp.cumsum(log_f, axis=1).transpose(0, 2, 1)
    outs = []
    for i in range(S // BLOCK_Q):
        q0, q1 = i * BLOCK_Q, (i + 1) * BLOCK_Q
        s = jnp.einsum('bqhd,bkhd->bhqk', q[:, q0:q1], k[:, :q1],
                       preferred_element_type=jnp.float32) * scale
        s = s + cum[:, :, q0:q1, None] - cum[:, :, None, :q1]
        causal = jnp.arange(q1)[None, :] <= jnp.arange(q0, q1)[:, None]
        s = jnp.where(causal, s, NEG_INF)
        w = jax.nn.softmax(s, axis=-1)
        outs.append(jnp.einsum('bhqk,bkhd->bqhd', w.astype(v.dtype), v[:, :q1]))
    return jnp.concatenate(outs, axis=1)

def _stick_breaking_attention(q, k, v):
    S, d = q.shape[1], q.shape[-1]
    scale = d ** -0.5
    outs = []
    for i in range(S // BLOCK_Q):
        q0, q1 = i * BLOCK_Q, (i + 1) * BLOCK_Q
        z = jnp.einsum('bqhd,bkhd->bhqk', q[:, q0:q1], k[:, :q1],
                       preferred_element_type=jnp.float32) * scale
        strict = jnp.arange(q1)[None, :] < jnp.arange(q0, q1)[:, None]
        log_1mb = jnp.where(strict, jax.nn.log_sigmoid(-z), 0.0)
        suffix = lax.cumsum(log_1mb, axis=3, reverse=True) - log_1mb
        a = jnp.where(strict, jnp.exp(jax.nn.log_sigmoid(z) + suffix), 0.0)
        outs.append(jnp.einsum('bhqk,bkhd->bqhd', a.astype(v.dtype), v[:, :q1]))
    return jnp.concatenate(outs, axis=1)

def _sliding_window_sink_attention(q, k, v, sinks):
    B, S, _, d = q.shape
    nb = S // WINDOW
    scale = d ** -0.5
    qb = q.reshape(B, nb, WINDOW, N_KV, GROUP, d)

    def band(x):
        xb = x.reshape(B, nb, WINDOW, N_KV, d)
        prev = jnp.concatenate([jnp.zeros_like(xb[:, :1]), xb[:, :-1]], axis=1)
        return jnp.concatenate([prev, xb], axis=2)

    kb, vb = band(k), band(v)
    s = jnp.einsum('bnqhgd,bnkhd->bnhgqk', qb, kb,
                   preferred_element_type=jnp.float32) * scale
    qi = jnp.arange(WINDOW)[:, None]
    kj = jnp.arange(2 * WINDOW)[None, :]
    rel = qi + WINDOW - kj
    valid = (rel >= 0) & (rel < WINDOW)
    first = (jnp.arange(nb)[:, None, None] == 0) & (kj[None] < WINDOW)
    mask = valid[None] & ~first
    s = jnp.where(mask[None, :, None, None], s, NEG_INF)
    sink = jnp.broadcast_to(
        sinks.astype(jnp.float32).reshape(N_KV, GROUP)[None, None, :, :, None, None],
        s.shape[:-1] + (1,))
    w = jax.nn.softmax(jnp.concatenate([s, sink], axis=-1), axis=-1)[..., :-1]
    o = jnp.einsum('bnhgqk,bnkhd->bnqhgd', w.astype(v.dtype), vb)
    return o.reshape(B, S, N_Q, d)

def _swiglu(x, w_gate, w_up, w_down):
    return (jax.nn.silu(x @ w_gate) * (x @ w_up)) @ w_down

def setup_inputs(seed: int = 0) -> dict:
    key = jax.random.key(seed)
    ks = jax.random.split(key, 20)
    f32 = jnp.float32

    def w(k, shape, fan_in):
        return jax.random.normal(k, shape, f32) * fan_in ** -0.5

    def gain(k, shape):
        return 1.0 + 0.02 * jax.random.normal(k, shape, f32)

    return {
        "x": jax.random.normal(ks[0], (BATCH, SEQ, D_MODEL), f32),
        "p": jax.random.normal(ks[1], (DEPTH, BATCH, SEQ, PLE_DIM), f32),
        "positions": jnp.broadcast_to(jnp.arange(SEQ, dtype=jnp.int32), (BATCH, SEQ)),
        "norm_mix": gain(ks[2], (DEPTH, D_MODEL)),
        "norm_ffn": gain(ks[3], (DEPTH, D_MODEL)),
        "norm_ple": gain(ks[4], (DEPTH, D_MODEL)),
        "norm_final": gain(ks[5], (D_MODEL,)),
        "ev_w_in": w(ks[6], (N_EVEN, D_MODEL, EVEN_IN), D_MODEL),
        "ev_b_f": 0.1 * jax.random.normal(ks[7], (N_EVEN, N_FOX), f32),
        "ev_w_out": w(ks[8], (N_EVEN, FOX_W + SB_W, D_MODEL), FOX_W + SB_W),
        "od_w_in": w(ks[9], (N_ODD, D_MODEL, ODD_IN), D_MODEL),
        "od_sinks": 0.5 * jax.random.normal(ks[10], (N_ODD, N_Q), f32),
        "od_w_out": w(ks[11], (N_ODD, N_Q * HEAD_DIM, D_MODEL), N_Q * HEAD_DIM),
        "ffn_w_gate": w(ks[12], (DEPTH, D_MODEL, D_FF), D_MODEL),
        "ffn_w_up": w(ks[13], (DEPTH, D_MODEL, D_FF), D_MODEL),
        "ffn_w_down": w(ks[14], (DEPTH, D_FF, D_MODEL), D_FF),
        "ple_w_proj": w(ks[15], (DEPTH, PLE_DIM, D_MODEL), PLE_DIM),
        "ple_w_gate": w(ks[16], (DEPTH, D_MODEL, D_MODEL), D_MODEL),
    }

def reference(x, p, positions, norm_mix, norm_ffn, norm_ple, norm_final,
              ev_w_in, ev_b_f, ev_w_out, od_w_in, od_sinks, od_w_out,
              ffn_w_gate, ffn_w_up, ffn_w_down, ple_w_proj, ple_w_gate):
    B, S, _ = x.shape
    h = x
    for i in range(DEPTH):
        hn = _rmsnorm(h, norm_mix[i])
        if i % 2 == 0:
            j = i // 2
            proj = hn @ ev_w_in[j]
            c = [0, FOX_W, 2 * FOX_W, 3 * FOX_W,
                 3 * FOX_W + SB_W, 3 * FOX_W + 2 * SB_W, 3 * FOX_W + 3 * SB_W]
            qa = proj[..., c[0]:c[1]].reshape(B, S, N_FOX, HEAD_DIM)
            ka = proj[..., c[1]:c[2]].reshape(B, S, N_FOX, HEAD_DIM)
            va = proj[..., c[2]:c[3]].reshape(B, S, N_FOX, HEAD_DIM)
            qs = proj[..., c[3]:c[4]].reshape(B, S, N_SB, HEAD_DIM)
            ks_ = proj[..., c[4]:c[5]].reshape(B, S, N_SB, HEAD_DIM)
            vs = proj[..., c[5]:c[6]].reshape(B, S, N_SB, HEAD_DIM)
            log_f = jax.nn.log_sigmoid(
                (proj[..., c[6]:] + ev_b_f[j]).astype(jnp.float32))
            o_fox = _forgetting_attention(qa, ka, va, log_f)
            o_sb = _stick_breaking_attention(qs, ks_, vs)
            mix = jnp.concatenate([o_fox.reshape(B, S, FOX_W),
                                   o_sb.reshape(B, S, SB_W)], axis=-1) @ ev_w_out[j]
        else:
            j = i // 2
            proj = hn @ od_w_in[j]
            qw, kw = N_Q * HEAD_DIM, N_KV * HEAD_DIM
            q = _rope(proj[..., :qw].reshape(B, S, N_Q, HEAD_DIM), positions)
            k = _rope(proj[..., qw:qw + kw].reshape(B, S, N_KV, HEAD_DIM), positions)
            v = proj[..., qw + kw:].reshape(B, S, N_KV, HEAD_DIM)
            o = _sliding_window_sink_attention(q, k, v, od_sinks[j])
            mix = o.reshape(B, S, qw) @ od_w_out[j]
        h = h + mix
        h = h + _swiglu(_rmsnorm(h, norm_ffn[i]), ffn_w_gate[i], ffn_w_up[i], ffn_w_down[i])
        gate = jax.nn.sigmoid(_rmsnorm(h, norm_ple[i]) @ ple_w_gate[i])
        h = h + gate * (p[i] @ ple_w_proj[i])
    return _rmsnorm(h, norm_final)


_drawn_inputs = setup_inputs


def setup_inputs(seed=0):
    import zlib

    import numpy as np

    out = dict(_drawn_inputs(seed))
    spreads = {}
    factors = {'norm_mix': 3.612,
     'norm_ffn': 3.633,
     'norm_ple': 64.0,
     'norm_final': 7.325,
     'ev_b_f': 3.855,
     'od_sinks': 61.628}
    for name, (base, spread) in spreads.items():
        noise = np.random.default_rng([zlib.crc32(name.encode()), seed]).standard_normal(out[name].shape)
        drawn = base * np.exp(spread * noise) if base else spread * noise
        out[name] = __import__('jax').numpy.asarray(drawn.astype(out[name].dtype))
    for name, factor in factors.items():
        out[name] = (out[name] * factor).astype(out[name].dtype)
    return out
```

```python
import math
from contextlib import ExitStack

import numpy as np

import concourse.bass as bass
from concourse import mybir

F32 = mybir.dt.float32
F32R = mybir.dt.float32r
BF16 = mybir.dt.bfloat16
I32 = mybir.dt.int32
ACT = mybir.ActivationFunctionType
ALU = mybir.AluOpType
AX_X = mybir.AxisListType.X

P = 128
NEG = -1e30
EPS = 1e-6
THETA = 10000.0
LOWEST = -3.0e38


def hybrid_trunk(nc, x, p, positions, norm_mix, norm_ffn, norm_ple, norm_final, ev_w_in, ev_b_f, ev_w_out,
                 od_w_in, od_sinks, od_w_out, ffn_w_gate, ffn_w_up, ffn_w_down, ple_w_proj, ple_w_gate, out):
    _, SEQ, DM = x.shape
    DEPTH = p.shape[0]
    PLE = p.shape[3]
    DFF = ffn_w_gate.shape[2]
    HD = 64
    HALF = HD // 2
    NFOX = ev_b_f.shape[1]
    NHEADS = DM // HD
    FOXW = NFOX * HD
    SBW = DM - FOXW
    NQ = od_sinks.shape[1]
    NKV = (od_w_in.shape[2] - NQ * HD) // (2 * HD)
    SCALE = HD ** -0.5
    KT = DM // P
    TB = SEQ // P
    CW = 256
    CHUNK = KT * CW
    FF2 = DFF // CW
    FT = DFF // P
    assert (SEQ, DM, DEPTH, PLE, DFF, NFOX, NQ, NKV) == (512, 1024, 2, 256, 2816, 8, 16, 4)

    KB = 1024
    base = (nc.sbuf_base + 63) // 64 * 64

    def at(name, shape, dt, kb):
        return nc.alloc_sbuf_tensor_at(name, shape, dt, offset=base + int(kb * KB))

    h = at("h", [P, KT, SEQ], F32, 0)
    x_hi = at("x_hi", [P, KT, SEQ], F32R, 16)
    x_lo = at("x_lo", [P, KT, SEQ], F32R, 32)
    w_raw = at("w_raw", [P, 2, CHUNK], F32, 48)
    w_hi = at("w_hi", [P, 2, CHUNK], F32R, 64)
    w_lo = at("w_lo", [P, 2, CHUNK], F32R, 80)
    X = 96
    act_hi = at("act_hi", [P, FT * SEQ], F32R, X)
    act_lo = at("act_lo", [P, FT * SEQ], F32R, X + 44)
    o_hi = at("o_hi", [P, KT, SEQ], F32R, X)
    o_lo = at("o_lo", [P, KT, SEQ], F32R, X + 16)
    v_nat = at("v_nat", [P, 2, TB, CW], F32, X + 32)
    gate_f = at("gate_f", [NFOX, SEQ], F32, X + 40)
    gate_t = at("gate_t", [NFOX, SEQ], F32, X + 42)
    gate_cum = at("gate_cum", [NFOX, SEQ], F32, X + 44)
    gate_zero = at("gate_zero", [NFOX, SEQ], F32, X + 46)
    q_pair = at("q_pair", [P, 4, SEQ], F32, X + 48)
    k_pad = at("k_pad", [P, 4, 2, SEQ], F32, X + 56)
    x_nat = at("x_nat", [P, TB, DM], F32, X + 72)
    f_keys = at("f_keys", [P, NFOX, SEQ], F32, X + 72)
    q1_pair = at("q1_pair", [P, NQ // 2, SEQ], F32, X + 32)
    k1_pad = at("k1_pad", [P, NKV, 2, SEQ], F32, X + 48)
    v1_dup = at("v1_dup", [P, TB, NKV, 2, HD], F32, X + 64)
    p1 = at("p1", [P, 2, TB, 2 * P], F32, X + 72)
    p1_t = at("p1_t", [P, 2, TB * 2 * P], F32, X + 80)
    xp_hi = at("xp_hi", [P, KT, SEQ], F32R, X)
    xp_lo = at("xp_lo", [P, KT, SEQ], F32R, X + 16)
    emb = at("emb", [P, KT, SEQ], F32, X + 44)
    pt_hi = at("pt_hi", [P, 2, SEQ], F32R, X + 60)
    pt_lo = at("pt_lo", [P, 2, SEQ], F32R, X + 64)
    p_nat = at("p_nat", [P, TB, PLE], F32, X + 68)
    gain_final = at("gain_final", [P, DM], F32, X + 76)
    result = at("result", [P, 2 * TB, SEQ], F32, X)
    C = 184
    ident = at("ident", [P, P], F32, C)
    neg_tri = at("neg_tri", [P, P], F32, C + 0.5)
    neg_ones = at("neg_ones", [P, P], F32, C + 1)
    ones = at("ones", [P, P], F32, C + 1.5)
    ident_b = at("ident_b", [P, P], BF16, C + 2)
    mask_qk = at("mask_qk", [P, P], BF16, C + 2.25)
    mask_kq = at("mask_kq", [P, P], BF16, C + 2.5)
    mask_win = at("mask_win", [P, 4, P], BF16, C + 2.75)
    mask_win0 = at("mask_win0", [P, 4, P], BF16, C + 3.75)
    r_tok = at("r_tok", [P, SEQ], F32, C + 4.75)
    cos_t = at("cos_t", [P, TB, 2, HALF], F32, C + 6.75)
    sin_t = at("sin_t", [P, TB, 2, HALF], F32, C + 7.75)
    gain_t = at("gain_t", [P, P], F32, C + 8.75)
    inv_freq = at("inv_freq", [P, HALF], F32, C + 9.25)
    small = at("small", [P, 160], F32, C + 9.375)
    pos_i = at("pos_i", [P, TB], I32, C + 10)
    minus_half = small[:, 0:4]
    r_col = small[:, 4:32]
    mean_sq = small[:, 32:36]
    ssq0 = small[:, 36:40]
    gate_bias = small[0:NFOX, 40:41]
    sinks = small[:, 44:60]
    sinks8 = small[:, 60:76]
    row_max = small[:, 76:84]
    neg_max = small[:, 84:92]
    row_sum = small[:, 92:100]
    row_inv = small[:, 100:108]
    sink_exp = small[:, 108:116]
    den = small[:, 116:124]
    pos_f = small[:, 124:128]
    W = 194.125
    B = [at(f"score_{i}", [P, 1280], F32, W + 5 * i) for i in range(5)]
    gains_nat = at("gains_nat", [P, P], F32, W)
    diag = at("diag", [P, TB, P], F32, W + 22)
    gs = at("gs", [P, 2, SEQ], F32, W)
    up = at("up", [P, 2, SEQ], F32, W + 4)
    sq = at("sq", [P, 2, SEQ], F32, W + 8)
    sq_sum = at("sq_sum", [P, SEQ], F32, W + 12)
    ple_t = at("ple_t", [P, 2, SEQ], F32, W + 14)
    x_sq = at("x_sq", [P, DM], F32, W + 10)
    ang = at("ang", [P, 2, TB, HALF], F32, W + 18)
    turns_i = at("turns_i", [P, 2, TB, HALF], I32, W + 19)
    turns = at("turns", [P, 2, TB, HALF], F32, W + 20)
    trig = at("trig", [P, 2, TB, HALF], F32, W + 21)
    rope_a = at("rope_a", [P, CW], F32, W)
    rope_b = at("rope_b", [P, CW], F32, W + 1)
    rope_q = at("rope_q", [P, CW], F32, W + 2)
    rope_k = at("rope_k", [P, NKV, 2, HD], F32, W + 3)

    f_dram = nc.dram_tensor("forget_cumsum", (NFOX, SEQ), F32).ap()

    OFF = [0, 512, 1024, 896]
    LEN = [(TB - b) * P for b in range(TB)]

    def cols(w, c0):
        return w.rearrange("(k q) n -> q k n", q=P)[:, :, c0:c0 + CW]

    def rows(w, k0):
        return w.rearrange("(k q) n -> q k n", q=P)[:, k0:k0 + 2, :]

    w_in0, w_in1 = ev_w_in[0], od_w_in[0]
    SB0 = 3 * FOXW
    GROUPS = [(SB0 + CW * g, SB0 + 2 * SBW + CW * g, SB0 + SBW + CW * g) for g in range(2)]
    GROUPS += [(CW * g, 2 * FOXW + CW * g, FOXW + CW * g) for g in range(2)]
    GROUP_CHUNK = [0, 4, 7, 10]
    GATE_CHUNK = 3
    N_OUT = [13, 61]
    N_FFN = [17, 65]
    N_DOWN = [n + 2 * FF2 for n in N_FFN]
    N_PLE = [n + FF2 for n in N_DOWN]
    N_IN1 = N_PLE[0] + 5
    N_ALL = N_PLE[1] + 5
    assert N_IN1 == 55 and N_IN1 + 6 == N_OUT[1] and N_ALL == 103

    with ExitStack() as ctx:
        def sem(name):
            return ctx.enter_context(nc.semaphore(name))

        ps = ctx.enter_context(nc.psum_tensor("ps", [P, 8, 512], F32))
        ps_flat = ps[:, :, :].rearrange("q b n -> q (b n)")
        z = [ps_flat[:, (2 + 3 * k) * 512:(2 + 3 * k) * 512 + 1280] for k in range(2)]

        x_in = [sem(f"x_in_{t}") for t in range(TB)]
        gains_in, small_in = sem("gains_in"), [sem(f"small_in_{i}") for i in range(3)]
        slot_in = [sem(f"slot_in_{i}") for i in range(2)]
        gate_cols_in = sem("gate_cols_in")
        p_in, gain_in = [sem(f"p_in_{i}") for i in range(2)], sem("gain_in")
        f_out, f_in = sem("f_out"), sem("f_in")
        out_sem = sem("out_sem")
        consts = sem("consts")
        k_zeroed, k1_zeroed = sem("k_zeroed"), sem("k1_zeroed")
        w_hi_done, w_lo_done = sem("w_hi_done"), sem("w_lo_done")
        h_done, x_hi_done, x_lo_done = sem("h_done"), sem("x_hi_done"), sem("x_lo_done")
        xt_ready = sem("xt_ready")
        gains_t_ready, gains_t_done = sem("gains_t_ready"), sem("gains_t_done")
        delta_ready = sem("delta_ready")
        sq_done, sq_sum_done, x_sq_done = sem("sq_done"), sem("sq_sum_done"), sem("x_sq_done")
        ssq_ready, mean_done, r_done = sem("ssq_ready"), sem("mean_done"), sem("r_done")
        diag_done, r_bc_ready, r_bc_done = sem("diag_done"), sem("r_bc_ready"), sem("r_bc_done")
        qk_ready, qk_done, v_ready, v_done = sem("qk_ready"), sem("qk_done"), sem("v_ready"), sem("v_done")
        gate_ready, gate_step = sem("gate_ready"), sem("gate_step")
        gate_abs = sem("gate_abs")
        z_ready, sb_abs, sb_l, c_ready = sem("z_ready"), sem("sb_abs"), sem("sb_l"), sem("c_ready")
        fx_max, fx_neg, fx_exp, fx_inv, fx_norm = (sem(n) for n in ("fx_max", "fx_neg", "fx_exp", "fx_inv", "fx_norm"))
        fx_t_ready, wt_done = sem("fx_t_ready"), sem("wt_done")
        pv_ready, o_hi_done, o_lo_done = sem("pv_ready"), sem("o_hi_done"), sem("o_lo_done")
        trig_step, trig_done, rope_angle = sem("trig_step"), sem("trig_done"), sem("rope_angle")
        in_ready, rope_step, rope_done, v1_done = sem("in_ready"), sem("rope_step"), sem("rope_done"), sem("v1_done")
        tr_ready, tr_done, table_step = sem("tr_ready"), sem("tr_done"), sem("table_step")
        s_ready, s_max, s_neg, s_exp, s_den, s_inv, s_norm = (
            sem(n) for n in ("s_ready", "s_max", "s_neg", "s_exp", "s_den", "s_inv", "s_norm"))
        t1_ready, t1_done, pv1_ready, o1_hi_done, o1_lo_done = (
            sem(n) for n in ("t1_ready", "t1_done", "pv1_ready", "o1_hi_done", "o1_lo_done"))
        L = range(DEPTH)
        g_ready, u_ready, g_done, u_done = ([sem(f"{n}_{i}") for i in L] for n in ("g_ready", "u_ready", "g_done", "u_done"))
        silu_done, a_done, a_hi_done, a_lo_done = (
            [sem(f"{n}_{i}") for i in L] for n in ("silu_done", "a_done", "a_hi_done", "a_lo_done"))
        down_used = [sem(f"down_used_{i}") for i in L]
        pt_ready, pt_hi_done, pt_lo_done = ([sem(f"{n}_{i}") for i in L] for n in ("pt_ready", "pt_hi_done", "pt_lo_done"))
        e_ready, e_done, pg_ready, pg_done = ([sem(f"{n}_{i}") for i in L] for n in ("e_ready", "e_done", "pg_ready", "pg_done"))
        sig_done, d_done = ([sem(f"{n}_{i}") for i in L] for n in ("sig_done", "d_done"))
        fin_ready, fin_done = sem("fin_ready"), sem("fin_done")

        V_MIX, V_FFN, V_PLE = [1, 4], [2, 5], [3, 6]
        DELTA = {1: 0, 2: 8, 4: 16, 5: 24}

        def bank1(idx):
            return idx % 2 if idx < 15 else 0

        def spreads(v):
            return v + 1 if v < 3 else v

        def last_product(n):
            for g, n0 in enumerate(GROUP_CHUNK):
                if n == n0:
                    return qk_ready, 4 * g + 2
                if n == n0 + 1:
                    return v_ready, 4 * g + 4
                if n == n0 + 2:
                    return qk_ready, 4 * g + 4
            if n == GATE_CHUNK:
                return gate_ready, 1
            for i in L:
                if N_OUT[i] <= n < N_OUT[i] + 4:
                    return delta_ready, DELTA[V_MIX[i]] + 2 * (n - N_OUT[i]) + 2
                if N_FFN[i] <= n < N_DOWN[i]:
                    c, u = divmod(n - N_FFN[i], 2)
                    return (u_ready if u else g_ready)[i], 2 * c + 2
                if N_DOWN[i] <= n < N_DOWN[i] + FF2 - 1:
                    return down_used[i], n - N_DOWN[i] + 1
                if n == N_DOWN[i] + FF2 - 1:
                    return delta_ready, DELTA[V_FFN[i]] + KT
                if n == N_PLE[i]:
                    return e_ready[i], KT
                if N_PLE[i] < n < N_PLE[i] + 5:
                    return pg_ready[i], 2 * (n - N_PLE[i])
            return in_ready, 4 * (n - N_IN1) + 4

        block = ctx.enter_context(nc.Block())

        @block.sync
        def _(sp):
            def load(n, src, it=0):
                if n >= 2:
                    sp.wait_ge(w_lo_done, n - 1 + 2 * it)
                k = src.shape[1]
                dst = w_raw[:, n % 2, :].rearrange("q (k n) -> q k n", k=k)
                sp.dma_start(dst, src).then_inc(slot_in[n % 2], 16)

            for t in range(TB):
                sp.dma_start(x_nat[:, t, :], x[0, t * P:(t + 1) * P, :]).then_inc(x_in[t], 16)
            for g, (q0, v0, k0) in enumerate(GROUPS):
                n = GROUP_CHUNK[g]
                load(n, cols(w_in0, q0))
                load(n + 1, cols(w_in0, v0))
                load(n + 2, cols(w_in0, k0))
                if g == 0:
                    sp.wait_ge(w_lo_done, GATE_CHUNK - 1)
                    dst = w_raw[:, GATE_CHUNK % 2, 0:KT * P].rearrange("q (k n) -> q k n", k=KT)
                    src = w_in0.rearrange("(k q) n -> q k n", q=P)
                    sp.dma_start(dst[:, :, NFOX:P], src[:, :, 0:P - NFOX]).then_inc(slot_in[GATE_CHUNK % 2], 16)
                    sp.dma_start(dst[:, :, 0:NFOX], src[:, :, SB0 + 3 * SBW:SB0 + 3 * SBW + NFOX]).then_inc(gate_cols_in, 16)
                if g == 1:
                    sp.wait_ge(gate_step, 4)
                    sp.dma_start(f_dram, gate_cum[:, :]).then_inc(f_out, 16)
                    sp.wait_ge(h_done, KT)
                    sp.wait_ge(x_sq_done, TB)
                    sp.wait_ge(f_out, 16)
                    for f in range(NFOX):
                        sp.dma_start(f_keys[:, f, :], f_dram[f:f + 1, :].broadcast_to([P, SEQ])).then_inc(f_in, 16)
            for i in L:
                if i == 1:
                    kv0 = NQ * HD
                    for c, c0 in enumerate([kv0, kv0 + CW] + [CW * j for j in range(4)]):
                        load(N_IN1 + c, cols(w_in1, c0))
                w_out = (ev_w_out, od_w_out)[i][0]
                for c in range(4):
                    load(N_OUT[i] + c, cols(w_out, CW * c))
                gate_v = ffn_w_gate[i].rearrange("(k q) n -> q k n", q=P)
                up_v = ffn_w_up[i].rearrange("(k q) n -> q k n", q=P)
                with sp.Fori(0, FF2) as c:
                    load(N_FFN[i], gate_v[:, :, bass.ds(c * CW, CW)], c)
                    load(N_FFN[i] + 1, up_v[:, :, bass.ds(c * CW, CW)], c)
                down_v = ffn_w_down[i].rearrange("(k q) n -> q k n", q=P)
                with sp.Fori(0, FF2 // 2) as c:
                    load(N_DOWN[i], down_v[:, bass.ds(c * 4, 2), :], c)
                    load(N_DOWN[i] + 1, down_v[:, bass.ds(c * 4 + 2, 2), :], c)
                load(N_DOWN[i] + FF2 - 1, rows(ffn_w_down[i], FT - 2))
                load(N_PLE[i], rows(ple_w_proj[i], 0))
                sp.wait_ge(down_used[i], FF2 - 1)
                sp.dma_start(p_nat[:, :, :], p[i, 0].rearrange("(t q) n -> q t n", q=P)).then_inc(p_in[i], 16)
                if i == 1:
                    sp.dma_start(gain_final[:, :], norm_final.rearrange("(a n) -> a n", a=1).broadcast_to([P, DM])).then_inc(gain_in, 16)
                for c in range(4):
                    load(N_PLE[i] + 1 + c, cols(ple_w_gate[i], CW * c))
            for j in range(2 * TB):
                half, t = divmod(j, TB)
                sp.wait_ge(fin_done, j + 1)
                sp.dma_start(out[0, t * P:(t + 1) * P, half * 512:(half + 1) * 512], result[:, j, :]).then_inc(out_sem, 16)
            sp.wait_ge(out_sem, 16 * 2 * TB)

        @block.gpsimd
        def _(pool):
            count = [0]

            def const(ins):
                count[0] += 1
                ins.then_inc(consts, 1)
                pool.wait_ge(consts, count[0])

            const(pool.memset(gains_nat[:, :], 0.0))
            const(pool.memset(ident[:, :], 0.0))
            const(pool.affine_select(out=ident[:, :], in_=ident[:, :], compare_op=ALU.not_equal, fill=1.0, base=0,
                                     pattern=[[-1, P]], channel_multiplier=1))
            const(pool.memset(minus_half, -0.5))
            const(pool.memset(ones[:, :], 1.0))
            const(pool.memset(neg_ones[:, :], -1.0))
            const(pool.affine_select(out=neg_tri[:, :], in_=neg_ones[:, :], compare_op=ALU.is_ge, fill=0.0, base=0,
                                     pattern=[[-1, P]], channel_multiplier=1))
            const(pool.memset(ident_b[:, :], 0.0))
            const(pool.affine_select(out=ident_b[:, :], in_=ident_b[:, :], compare_op=ALU.not_equal, fill=1.0, base=0,
                                     pattern=[[-1, P]], channel_multiplier=1))
            const(pool.memset(mask_win[:, :, :], 0.0))
            const(pool.affine_select(out=mask_kq[:, :], in_=mask_win[:, 0, :], compare_op=ALU.is_gt, fill=NEG, base=0,
                                     pattern=[[1, P]], channel_multiplier=-1))
            const(pool.affine_select(out=mask_qk[:, :], in_=mask_win[:, 0, :], compare_op=ALU.is_ge, fill=NEG, base=0,
                                     pattern=[[-1, P]], channel_multiplier=1))
            const(pool.memset(gate_zero[:, :], 0.0))
            for j in range(2):
                const(pool.tensor_copy(mask_win[:, 2 * j, :], mask_kq[:, :]))
                const(pool.tensor_copy(mask_win[:, 2 * j + 1, :], mask_qk[:, :]))
            const(pool.memset(mask_win0[:, 0, :], NEG))
            const(pool.tensor_copy(mask_win0[:, 1:4, :], mask_win[:, 1:4, :]))
            for half in range(2):
                pool.memset(k_pad[64 * (1 - half):64 * (2 - half), :, half, :], 0.0).then_inc(k_zeroed, 1)
                pool.wait_ge(k_zeroed, half + 1)
            for j in range(HALF):
                value = float(np.float32(THETA) ** np.float32(-j / HALF))
                const(pool.memset(inv_freq[:, j:j + 1], value))

            def factor(v):
                pool.wait_ge(mean_done, v + 1)
                pool.tensor_tensor(r_col[:, 4 * v:4 * v + 4], mean_sq, minus_half, ALU.pow).then_inc(r_done, 1)

            def add_squares(v):
                for m in range(1, KT):
                    pool.wait_ge(sq_done, KT * (v - 1) + m + 1)
                    if m > 1:
                        pool.wait_ge(sq_sum_done, (KT - 1) * (v - 1) + m - 1)
                    pool.tensor_tensor(sq_sum[:, :], sq_sum[:, :], sq[:, m % 2, :], ALU.add).then_inc(sq_sum_done, 1)

            def hidden(i, c):
                for j in range(2):
                    pool.wait_ge(silu_done[i], c * 2 + j + 1)
                    pool.wait_ge(u_done[i], c * 2 + j + 1)
                    pool.tensor_tensor(up[:, j, :], gs[:, j, :], up[:, j, :], ALU.mult).then_inc(a_done[i], 1)
                    pool.wait_ge(a_hi_done[i], c * 2 + j + 1)
                    pool.tensor_tensor(act_lo[:, bass.ds((c * 2 + j) * SEQ, SEQ)], up[:, j, :],
                                       act_hi[:, bass.ds((c * 2 + j) * SEQ, SEQ)].bitcast(F32), ALU.subtract).then_inc(a_lo_done[i], 1)

            factor(0)
            for i in L:
                if i == 1:
                    pool.wait_ge(r_done, 4)
                    for half in range(2):
                        pool.memset(k1_pad[64 * (1 - half):64 * (2 - half), :, half, :], 0.0).then_inc(k1_zeroed, 1)
                        pool.wait_ge(k1_zeroed, half + 1)
                add_squares(V_MIX[i])
                factor(V_MIX[i])
                with pool.Fori(0, FF2) as c:
                    hidden(i, c)
                add_squares(V_FFN[i])
                factor(V_FFN[i])
                for m in range(KT):
                    pool.wait_ge(sig_done[i], m + 1)
                    pool.tensor_tensor(ple_t[:, m % 2, :], ple_t[:, m % 2, :], emb[:, m, :], ALU.mult).then_inc(d_done[i], 1)
                    if m >= 2:
                        v = V_PLE[i]
                        pool.wait_ge(sq_done, KT * (v - 1) + m)
                        if m > 2:
                            pool.wait_ge(sq_sum_done, (KT - 1) * (v - 1) + m - 2)
                        pool.tensor_tensor(sq_sum[:, :], sq_sum[:, :], sq[:, (m - 1) % 2, :], ALU.add).then_inc(sq_sum_done, 1)
                v = V_PLE[i]
                pool.wait_ge(sq_done, KT * v)
                pool.wait_ge(sq_sum_done, (KT - 1) * (v - 1) + KT - 2)
                pool.tensor_tensor(sq_sum[:, :], sq_sum[:, :], sq[:, (KT - 1) % 2, :], ALU.add).then_inc(sq_sum_done, 1)
                factor(V_PLE[i])

        @block.scalar
        def _(act):
            def split_hi(n, it=0, done=None):
                act.wait_ge(slot_in[n % 2], (n // 2 + it + 1) * 16)
                if n == GATE_CHUNK:
                    act.wait_ge(gate_cols_in, 16)
                if done is None and n >= 2:
                    done = last_product(n - 2)
                if done is not None:
                    act.wait_ge(*done)
                size = KT * P if n == GATE_CHUNK else CHUNK
                act.activation(w_hi[:, n % 2, 0:size], w_raw[:, n % 2, 0:size], ACT.Copy).then_inc(w_hi_done, 1)

            def gained(v, m, hi):
                act.wait_ge(h_done, KT * v + m + 1)
                norm = {0: 0, 1: 2, 2: 4, 3: 1, 4: 3, 5: 5}[v]
                act.activation(hi[:, m, :], h[:, m, :], ACT.Copy, scale=gain_t[:, norm * KT + m:norm * KT + m + 1]).then_inc(x_hi_done, 1)

            def square(v, m):
                act.wait_ge(h_done, KT * v + m + 1)
                if m > 2:
                    act.wait_ge(sq_sum_done, (KT - 1) * (v - 1) + m - 2)
                dst = sq[:, m % 2, :] if m else sq_sum[:, :]
                act.activation(dst, h[:, m, :], ACT.Square).then_inc(sq_done, 1)

            def keep_factor(v):
                act.wait_ge(r_bc_ready, spreads(v))
                act.activation(r_tok[:, :], ps[:, 6, :], ACT.Copy).then_inc(r_bc_done, 1)

            def keep_v(g, t):
                act.wait_ge(v_ready, 4 * g + t + 1)
                act.wait_ge(r_done, 1)
                act.activation(v_nat[:, g % 2, t, :], ps[:, 0 if g else 1, 0:CW], ACT.Copy, scale=r_col[:, t:t + 1]).then_inc(v_done, 1)

            act.preload_act_table_set("natural_log_exp_and_others")
            act.wait_ge(consts, 1)
            for j, gains in enumerate((norm_mix, norm_ffn, norm_ple)):
                act.dma_start(gains_nat[2 * KT * j:2 * KT * (j + 1), :], gains.rearrange("l (k n) -> (l k) n", n=P)).then_inc(gains_in, 16)
            act.dma_start(gate_bias, ev_b_f.rearrange("a f -> f a"), allow_slow_non_contiguous=True).then_inc(small_in[0], 16)
            act.dma_start(sinks, od_sinks.broadcast_to([P, NQ])).then_inc(small_in[1], 16)
            act.dma_start(pos_i[:, :], positions.rearrange("a (t q) -> q (a t)", q=P), allow_slow_non_contiguous=True).then_inc(small_in[2], 16)
            for t in range(TB):
                act.wait_ge(x_in[t], 16)
                if t:
                    act.wait_ge(x_sq_done, t)
                act.activation(x_sq[:, :], x_nat[:, t, :], ACT.Square, accum_out=ssq0[:, t:t + 1]).then_inc(x_sq_done, 1)
            act.wait_ge(gains_t_done, 1)
            gained(0, 0, x_hi)
            split_hi(0)
            for m in range(1, KT):
                gained(0, m, x_hi)
            split_hi(1)
            keep_factor(0)

            for t in range(TB):
                keep_v(0, t)
                if t == 1:
                    split_hi(2)
            split_hi(3)
            split_hi(4)
            act.wait_ge(gate_step, 2)
            act.activation(gate_t[:, :], gate_f[:, :], ACT.Abs).then_inc(gate_abs, 1)
            act.wait_ge(gate_abs, 1)
            act.activation(gate_t[:, :], gate_t[:, :], ACT.Exp, scale=-1.0).then_inc(gate_abs, 1)
            act.wait_ge(gate_abs, 2)
            act.activation(gate_t[:, :], gate_t[:, :], ACT.Ln, bias=1.0).then_inc(gate_abs, 1)
            split_hi(5)

            def front(s):
                buf = B[s % 2]
                if s < 8:
                    act.wait_ge(z_ready, s + 1)
                    act.activation(buf[:, :], z[s % 2], ACT.Abs).then_inc(sb_abs, 1)
                    act.wait_ge(sb_abs, 3 * s + 1)
                    act.activation(buf[:, :], buf[:, :], ACT.Exp, scale=-1.0).then_inc(sb_abs, 1)
                    act.wait_ge(sb_abs, 3 * s + 2)
                    act.activation(buf[:, :], buf[:, :], ACT.Ln, bias=1.0).then_inc(sb_abs, 1)
                else:
                    act.wait_ge(fx_neg, s - 7)
                    for b in range(TB):
                        q = TB - 1 - b
                        part = buf[:, OFF[b]:OFF[b] + LEN[b]]
                        act.activation(part, part, ACT.Exp, bias=neg_max[:, q:q + 1], accum_out=row_sum[:, q:q + 1]).then_inc(fx_exp, 1)

            def back(s):
                if s >= 2:
                    act.wait_ge(pv_ready, s - 1)
                if s < 8:
                    act.wait_ge(c_ready, s + 1)
                else:
                    act.wait_ge(fx_t_ready, s - 7)
                act.activation(B[3 + s % 2][:, :], z[s % 2], ACT.Exp if s < 8 else ACT.Copy).then_inc(wt_done, 1)

            def keep_output(s):
                r0, tile = 64 * (s % 2), (4 + s // 2) % 8
                act.wait_ge(pv_ready, s + 1)
                act.activation(o_hi[r0:r0 + 64, tile, :], ps[r0:r0 + 64, 1, :], ACT.Copy).then_inc(o_hi_done, 1)

            front(0)
            for s in range(NHEADS):
                g, i = divmod(s, 4)
                early = g < 3 and i < 3
                if early:
                    front(s + 1)
                back(s)
                if not early and s + 1 < NHEADS:
                    front(s + 1)
                if g < 3:
                    if i == 0 and s:
                        act.wait_ge(pv_ready, s)
                    keep_v(g + 1, i)
                    if i == 1:
                        split_hi(GROUP_CHUNK[g + 1] + 2)
                    if i == 3:
                        split_hi(GROUP_CHUNK[g + 1] + 3)
                        split_hi(GROUP_CHUNK[g + 1] + 4)
                if s:
                    keep_output(s - 1)
            keep_output(NHEADS - 1)

            for l in L:
                if l == 1:
                    def keep_transposed(u):
                        act.wait_ge(tr_ready, u + 1)
                        t = u % 4
                        if u < 4:
                            act.wait_ge(k1_zeroed, 2)
                            for half in range(2):
                                rs = slice(64 * half, 64 * half + 64)
                                ins = act.activation(k1_pad[rs, :, half, t * P:(t + 1) * P],
                                                     ps[rs, 6, :].rearrange("q (g n) -> q g n", g=NKV), ACT.Copy)
                            ins.then_inc(tr_done, 1)
                        else:
                            c = u // 4 - 1
                            act.activation(q1_pair[:, 2 * c:2 * c + 2, t * P:(t + 1) * P],
                                           ps[:, bank1(u + 4), CW:2 * CW].rearrange("q (g n) -> q g n", g=2), ACT.Copy).then_inc(tr_done, 1)

                    def weights(s):
                        act.wait_ge(s_neg, s + 1)
                        o = 4 * (s % 2)
                        for b in range(TB):
                            act.activation(p1[:, s % 2, b, :], ps[:, 2 + 2 * (s % 2) + b // 2, (b % 2) * 256:(b % 2) * 256 + 256], ACT.Exp,
                                           bias=neg_max[:, o + b:o + b + 1], scale=SCALE,
                                           accum_out=row_sum[:, o + b:o + b + 1]).then_inc(s_exp, 1)
                        act.activation(sink_exp[:, o:o + 4], neg_max[:, o:o + 4], ACT.Exp, bias=sinks[:, s:s + 1]).then_inc(s_exp, 1)

                    for idx in range(12):
                        if 4 <= idx < 8:
                            act.wait_ge(in_ready, idx + 1)
                            act.wait_ge(r_done, 4)
                            for d in range(2):
                                ins = act.activation(v1_dup[:, idx - 4, :, d, :], ps[:, idx % 2, 0:CW].rearrange("q (g n) -> q g n", g=NKV),
                                                     ACT.Copy, scale=r_col[:, 12 + idx - 4:13 + idx - 4])
                            ins.then_inc(v1_done, 1)
                        else:
                            keep_transposed(idx if idx < 4 else idx - 4)
                        if idx % 4 == 3:
                            split_hi(N_IN1 + idx // 4 + 2)

                    def keep_output1(s):
                        r0 = 64 * (s % 2)
                        act.wait_ge(pv1_ready, s + 1)
                        act.activation(o_hi[r0:r0 + 64, s // 2, :], ps[r0:r0 + 64, 1, :], ACT.Copy).then_inc(o1_hi_done, 1)

                    weights(0)
                    keep_transposed(8)
                    weights(1)
                    keep_transposed(9)
                    for s in range(NQ):
                        act.wait_ge(t1_ready, s + 1)
                        if s >= 2:
                            act.wait_ge(pv1_ready, s - 1)
                        act.activation(p1_t[:, s % 2, 0:7 * P], ps_flat[:, 6 * 512:6 * 512 + 7 * P], ACT.Copy).then_inc(t1_done, 1)
                        if s < 10:
                            keep_transposed(10 + s)
                        if s + 2 < NQ:
                            weights(s + 2)
                        keep_output1(s)
                        if s < 9 and s % 4 == 0:
                            split_hi(N_IN1 + (15 + s) // 4 + 2)
                for m in range(KT):
                    gained(V_MIX[l], m, x_hi)
                    square(V_MIX[l], m)
                    if m % 2:
                        split_hi(N_OUT[l] + m // 2 + 2)
                act.preload_act_table_set("silu_and_others")
                if l == 0:
                    act.wait_ge(trig_step, 1)
                    act.activation(trig[:, :, :, :], ang[:, :, :, :], ACT.Sin).then_inc(trig_done, 1)
                keep_factor(V_MIX[l])

                def hidden(i, c):
                    for j in range(2):
                        act.wait_ge(g_done[i], c * 2 + j + 1)
                        act.activation(gs[:, j, :], gs[:, j, :], ACT.Silu).then_inc(silu_done[i], 1)
                    split_hi(N_FFN[i] + 2, c, (g_ready[i], c * 2 + 2))
                    for j in range(2):
                        act.wait_ge(a_done[i], c * 2 + j + 1)
                        act.activation(act_hi[:, bass.ds((c * 2 + j) * SEQ, SEQ)], up[:, j, :], ACT.Copy).then_inc(a_hi_done[i], 1)
                    split_hi(N_FFN[i] + 3, c, (u_ready[i], c * 2 + 2))

                with act.Fori(0, FF2) as c:
                    hidden(l, c)
                with act.Fori(0, FF2 // 2) as c:
                    split_hi(N_DOWN[l] + 2, c, (down_used[l], c * 2 + 1))
                    split_hi(N_DOWN[l] + 3, c, (down_used[l], c * 2 + 2))
                for m in range(KT):
                    gained(V_FFN[l], m, xp_hi)
                    square(V_FFN[l], m)
                for j in range(2):
                    act.wait_ge(pt_ready[l], j + 1)
                    act.activation(pt_hi[:, j, :], ps[:, j, :], ACT.Copy).then_inc(pt_hi_done[l], 1)
                split_hi(N_PLE[l] + 1)
                for m in range(KT):
                    act.wait_ge(e_ready[l], m + 1)
                    act.activation(emb[:, m, :], ps[:, 2 + m % 2, :], ACT.Copy).then_inc(e_done[l], 1)
                split_hi(N_PLE[l] + 2)
                keep_factor(V_FFN[l])
                for m in range(KT):
                    act.wait_ge(pg_done[l], m + 1)
                    act.activation(ple_t[:, m % 2, :], ple_t[:, m % 2, :], ACT.Sigmoid).then_inc(sig_done[l], 1)
                    if m % 2 and N_PLE[l] + 3 + m // 2 < N_ALL:
                        split_hi(N_PLE[l] + 3 + m // 2)
                    if m:
                        if l == 0:
                            gained(3, m - 1, x_hi)
                        square(V_PLE[l], m - 1)
                if l == 0:
                    gained(3, KT - 1, x_hi)
                square(V_PLE[l], KT - 1)
                if l == 0:
                    act.preload_act_table_set("natural_log_exp_and_others")

        @block.vector
        def _(dve):
            def split_lo(n, it=0):
                dve.wait_ge(w_hi_done, n + 1 + 2 * it)
                size = KT * P if n == GATE_CHUNK else CHUNK
                dve.tensor_tensor(w_lo[:, n % 2, 0:size], w_raw[:, n % 2, 0:size], w_hi[:, n % 2, 0:size].bitcast(F32),
                                  ALU.subtract).then_inc(w_lo_done, 1)

            def gained_lo(v, m, hi, lo):
                dve.wait_ge(x_hi_done, KT * v + m + 1)
                norm = {0: 0, 1: 2, 2: 4, 3: 1, 4: 3, 5: 5}[v]
                dve.scalar_tensor_tensor(out=lo[:, m, :], in0=h[:, m, :], scalar=gain_t[:, norm * KT + m:norm * KT + m + 1],
                                         in1=hi[:, m, :].bitcast(F32), op0=ALU.mult, op1=ALU.subtract).then_inc(x_lo_done, 1)

            def mean(v, src):
                dve.tensor_scalar(mean_sq, src, 1.0 / DM, EPS, ALU.mult, ALU.add).then_inc(mean_done, 1)

            def factor(v):
                if v:
                    dve.wait_ge(ssq_ready, v)
                    mean(v, ps[:, 7, 0:TB])
                dve.wait_ge(r_done, v + 1)
                if v == 3:
                    return
                for t in range(TB):
                    ins = dve.tensor_scalar(diag[:, t, :], ident[:, :], r_col[:, 4 * v + t:4 * v + t + 1], None, ALU.mult)
                ins.then_inc(diag_done, 1)

            def add_delta(v, m, bank):
                dve.wait_ge(delta_ready, DELTA[v] + m + 1)
                dve.tensor_tensor(h[:, m, :], ps[:, bank, :], h[:, m, :], ALU.add).then_inc(h_done, 1)

            def keep_qk(g, j):
                slot = (2 * g + j % 2) % 4
                dve.wait_ge(qk_ready, 4 * g + j + 1)
                if j < 2:
                    dve.scalar_tensor_tensor(out=q_pair[:, slot, :], in0=ps[:, 0, :], scalar=SCALE, in1=r_tok[:, :],
                                             op0=ALU.mult, op1=ALU.mult).then_inc(qk_done, 1)
                else:
                    for half in range(2):
                        rs = slice(64 * half, 64 * half + 64)
                        ins = dve.tensor_tensor(k_pad[rs, slot, half, :], ps[rs, 0, :], r_tok[rs, :], ALU.mult)
                    ins.then_inc(qk_done, 1)

            dve.wait_ge(gains_t_ready, 1)
            dve.tensor_copy(gain_t[:, :], ps[:, 0, 0:P]).then_inc(gains_t_done, 1)
            dve.wait_ge(gains_t_done, 1)
            for m in range(KT):
                dve.wait_ge(xt_ready, m + 1)
                dve.tensor_copy(h[:, m, :], ps[:, 2 + m % 4, :]).then_inc(h_done, 1)
                if m == 1:
                    dve.wait_ge(x_sq_done, TB)
                    mean(0, ssq0)
                if m == 3:
                    factor(0)
                if m:
                    gained_lo(0, m - 1, x_hi, x_lo)
                if m == 5:
                    split_lo(0)
            gained_lo(0, KT - 1, x_hi, x_lo)
            split_lo(1)

            dve.wait_ge(k_zeroed, 2)
            dve.wait_ge(r_bc_done, 1)
            for j in range(4):
                keep_qk(0, j)
                if j == 1:
                    split_lo(2)
            split_lo(3)
            split_lo(4)
            dve.wait_ge(gate_ready, 1)
            dve.tensor_tensor(gate_f[:, :], ps[0:NFOX, 7, :], r_tok[0:NFOX, :], ALU.mult).then_inc(gate_step, 1)
            dve.wait_ge(gate_step, 1)
            dve.wait_ge(small_in[0], 16)
            dve.tensor_scalar(gate_f[:, :], gate_f[:, :], gate_bias, None, ALU.add).then_inc(gate_step, 1)
            dve.wait_ge(gate_step, 2)
            dve.wait_ge(gate_abs, 3)
            dve.scalar_tensor_tensor(out=gate_f[:, :], in0=gate_f[:, :], scalar=0.0, in1=gate_t[:, :],
                                     op0=ALU.min, op1=ALU.subtract).then_inc(gate_step, 1)
            dve.wait_ge(gate_step, 3)
            dve.wait_ge(consts, 13)
            dve.tensor_tensor_scan(gate_cum[:, :], gate_f[:, :], gate_zero[:, :], 0.0, ALU.add, ALU.add).then_inc(gate_step, 1)
            split_lo(5)

            def front(s):
                zs, buf = z[s % 2], B[s % 2]
                if s < 8:
                    dve.wait_ge(sb_abs, 3 * s + 3)
                    if s:
                        dve.wait_ge(c_ready, s)
                    dve.scalar_tensor_tensor(out=B[2][:, :], in0=zs, scalar=0.0, in1=buf[:, :],
                                             op0=ALU.max, op1=ALU.add).then_inc(sb_l, 1)
                else:
                    f = s - 8
                    dve.wait_ge(z_ready, s + 1)
                    dve.wait_ge(f_in, 16 * NFOX)
                    for b in range(TB):
                        q = TB - 1 - b
                        dve.tensor_tensor_reduce(buf[:, OFF[b]:OFF[b] + LEN[b]], zs[:, OFF[b]:OFF[b] + LEN[b]], f_keys[:, f, 0:LEN[b]],
                                                 1.0, LOWEST, ALU.subtract, ALU.max, row_max[:, q:q + 1]).then_inc(fx_max, 1)
                    dve.wait_ge(fx_max, 4 * f + 4)
                    dve.tensor_scalar(neg_max[:, 0:4], row_max[:, 0:4], -1.0, None, ALU.mult).then_inc(fx_neg, 1)
                    dve.wait_ge(fx_exp, 4 * f + 4)
                    dve.reciprocal(row_inv[:, 0:4], row_sum[:, 0:4]).then_inc(fx_inv, 1)
                    dve.wait_ge(fx_inv, f + 1)
                    for b in range(TB):
                        q = TB - 1 - b
                        part = buf[:, OFF[b]:OFF[b] + LEN[b]]
                        ins = dve.tensor_scalar(part, part, row_inv[:, q:q + 1], None, ALU.mult)
                    ins.then_inc(fx_norm, 1)

            def keep_output_lo(s):
                r0, tile = 64 * (s % 2), (4 + s // 2) % 8
                dve.wait_ge(o_hi_done, s + 1)
                dve.tensor_tensor(o_lo[r0:r0 + 64, tile, :], ps[r0:r0 + 64, 1, :], o_hi[r0:r0 + 64, tile, :].bitcast(F32),
                                  ALU.subtract).then_inc(o_lo_done, 1)

            front(0)
            for s in range(NHEADS):
                g, i = divmod(s, 4)
                early = g < 3 and i < 3
                if early and g >= 2:
                    front(s + 1)
                if g < 3:
                    keep_qk(g + 1, i)
                if early and g < 2:
                    front(s + 1)
                if not early and s + 1 < NHEADS:
                    front(s + 1)
                if g < 3:
                    if i == 1:
                        split_lo(GROUP_CHUNK[g + 1] + 2)
                    if i == 3:
                        split_lo(GROUP_CHUNK[g + 1] + 3)
                        split_lo(GROUP_CHUNK[g + 1] + 4)
                if s:
                    keep_output_lo(s - 1)
            keep_output_lo(NHEADS - 1)

            for l in L:
                if l == 1:
                    factor(3)
                    for t in range(TB):
                        for table in (cos_t, sin_t):
                            ins = dve.tensor_scalar(table[:, t, :, :], table[:, t, :, :], r_col[:, 12 + t:13 + t], None, ALU.mult)
                    ins.then_inc(table_step, 1)
                    dve.wait_ge(table_step, 2)
                    dve.wait_ge(small_in[1], 16)
                    dve.tensor_scalar(sinks8, sinks, 1.0 / SCALE, None, ALU.mult).then_inc(table_step, 1)
                    dve.wait_ge(table_step, 3)

                    def rotate(idx):
                        u = idx if idx < 4 else idx - 4
                        t = idx % 4
                        dve.wait_ge(in_ready, idx + 1)
                        if u >= 1:
                            dve.wait_ge(tr_ready, u)
                        src = ps[:, bank1(idx), 0:CW].rearrange("q (g e n) -> q g e n", g=4, e=2)
                        a = rope_a[:, :].rearrange("q (g e n) -> q g e n", g=4, e=2)
                        b = rope_b[:, :].rearrange("q (g e n) -> q g e n", g=4, e=2)
                        for e in range(2):
                            dve.tensor_tensor(b[:, :, e, :], src[:, :, 1 - e, :], sin_t[:, t:t + 1, e, :].broadcast_to([P, 4, HALF]), ALU.mult)
                        for e in range(2):
                            ins = dve.tensor_tensor(a[:, :, e, :], src[:, :, e, :], cos_t[:, t:t + 1, e, :].broadcast_to([P, 4, HALF]), ALU.mult)
                        ins.then_inc(rope_step, 1)
                        dve.wait_ge(rope_step, u + 1)
                        if idx < 4:
                            for d in range(2):
                                ins = dve.tensor_tensor(rope_k[:, :, d, :], rope_a[:, :].rearrange("q (g n) -> q g n", g=4),
                                                        rope_b[:, :].rearrange("q (g n) -> q g n", g=4), ALU.add)
                        else:
                            ins = dve.tensor_tensor(rope_q[:, :], rope_a[:, :], rope_b[:, :], ALU.add)
                        ins.then_inc(rope_done, 1)

                    def maximum(s):
                        o = 4 * (s % 2)
                        dve.wait_ge(s_ready, s + 1)
                        b0 = 2 + 2 * (s % 2)
                        dve.tensor_reduce(row_max[:, o:o + 4], ps[:, b0:b0 + 2, :].rearrange("q b (c n) -> q (b c) n", c=2), AX_X, ALU.max).then_inc(s_max, 1)
                        dve.wait_ge(s_max, s + 1)
                        dve.tensor_scalar(neg_max[:, o:o + 4], row_max[:, o:o + 4], sinks8[:, s:s + 1], -SCALE, ALU.max, ALU.mult).then_inc(s_neg, 1)

                    def normalise(s):
                        o = 4 * (s % 2)
                        dve.wait_ge(s_exp, 5 * s + 5)
                        dve.tensor_tensor(den[:, o:o + 4], row_sum[:, o:o + 4], sink_exp[:, o:o + 4], ALU.add).then_inc(s_den, 1)
                        dve.wait_ge(s_den, s + 1)
                        dve.reciprocal(row_inv[:, o:o + 4], den[:, o:o + 4]).then_inc(s_inv, 1)
                        dve.wait_ge(s_inv, s + 1)
                        for b in range(TB):
                            ins = dve.tensor_scalar(p1[:, s % 2, b, :], p1[:, s % 2, b, :], row_inv[:, o + b:o + b + 1], None, ALU.mult)
                        ins.then_inc(s_norm, 1)

                    for idx in range(13):
                        if not 4 <= idx < 8:
                            rotate(idx)
                        if idx % 4 == 3:
                            split_lo(N_IN1 + idx // 4 + 2)
                    maximum(0)
                    rotate(13)
                    normalise(0)
                    maximum(1)
                    rotate(14)
                    normalise(1)

                    def keep_output1_lo(s):
                        r0 = 64 * (s % 2)
                        dve.wait_ge(o1_hi_done, s + 1)
                        dve.tensor_tensor(o_lo[r0:r0 + 64, s // 2, :], ps[r0:r0 + 64, 1, :], o_hi[r0:r0 + 64, s // 2, :].bitcast(F32),
                                          ALU.subtract).then_inc(o1_lo_done, 1)

                    for s in range(NQ):
                        if s + 2 < NQ:
                            maximum(s + 2)
                        keep_output1_lo(s)
                        if s + 2 < NQ:
                            normalise(s + 2)
                        if s < 9:
                            rotate(15 + s)
                            if s % 4 == 0:
                                split_lo(N_IN1 + (15 + s) // 4 + 2)
                v = V_MIX[l]
                for m in range(KT):
                    add_delta(v, m, 4 + m % 2)
                    if m:
                        gained_lo(v, m - 1, x_hi, x_lo)
                    if m % 2:
                        split_lo(N_OUT[l] + m // 2 + 2)
                gained_lo(v, KT - 1, x_hi, x_lo)
                factor(v)
                if l == 0:
                    steps = [0]

                    def step(ins):
                        steps[0] += 1
                        ins.then_inc(rope_angle, 1)
                        dve.wait_ge(rope_angle, steps[0])

                    dve.wait_ge(small_in[2], 16)
                    dve.wait_ge(consts, 51)
                    step(dve.tensor_copy(pos_f, pos_i[:, :]))
                    for e in range(2):
                        for t in range(TB):
                            ins = dve.tensor_scalar(ang[:, e, t, :], inv_freq[:, :], pos_f[:, t:t + 1], None, ALU.mult)
                    step(ins)
                    for e in range(2):
                        ins = dve.tensor_scalar(turns[:, e, :, :], ang[:, e, :, :], 1.0 / (2 * math.pi), 0.25 * e, ALU.mult, ALU.add)
                    step(ins)
                    step(dve.tensor_copy(turns_i[:, :, :, :], turns[:, :, :, :]))
                    step(dve.tensor_copy(turns[:, :, :, :], turns_i[:, :, :, :]))
                    two_pi = 2 * math.pi
                    part1 = 6.28125
                    part2 = math.floor((two_pi - part1) * 2 ** 20) / 2 ** 20
                    part3 = two_pi - part1 - part2
                    for part in (part1, part2, part3):
                        step(dve.scalar_tensor_tensor(out=ang[:, :, :, :].rearrange("q e t n -> q (e t n)"),
                                                      in0=turns[:, :, :, :].rearrange("q e t n -> q (e t n)"), scalar=-part,
                                                      in1=ang[:, :, :, :].rearrange("q e t n -> q (e t n)"), op0=ALU.mult, op1=ALU.add))
                    step(dve.tensor_scalar(ang[:, 1, :, :], ang[:, 1, :, :], math.pi / 2, None, ALU.add))
                    dve.tensor_scalar(ang[:, :, :, :], ang[:, :, :, :], 3.1415925, -3.1415925, ALU.min, ALU.max).then_inc(trig_step, 1)
                    dve.wait_ge(trig_done, 1)
                    for e in range(2):
                        dve.tensor_scalar(cos_t[:, :, e, :], trig[:, 1, :, :], 1.0, None, ALU.mult)
                        ins = dve.tensor_scalar(sin_t[:, :, e, :], trig[:, 0, :, :], 2.0 * e - 1.0, None, ALU.mult)
                    ins.then_inc(table_step, 1)
                dve.wait_ge(r_bc_done, spreads(v))

                def hidden(i, c, first):
                    for j in range(2):
                        dve.wait_ge(g_ready[i], c * 2 + j + 1)
                        if not first:
                            dve.wait_ge(a_done[i], c * 2 + j - 1)
                        dve.tensor_tensor(gs[:, j, :], ps[:, j, :], r_tok[:, :], ALU.mult).then_inc(g_done[i], 1)
                    split_lo(N_FFN[i] + 2, c)
                    for j in range(2):
                        dve.wait_ge(u_ready[i], c * 2 + j + 1)
                        if not first:
                            dve.wait_ge(a_lo_done[i], c * 2 + j - 1)
                        dve.tensor_tensor(up[:, j, :], ps[:, 2 + j, :], r_tok[:, :], ALU.mult).then_inc(u_done[i], 1)
                    split_lo(N_FFN[i] + 3, c)

                hidden(l, 0, True)
                with dve.Fori(1, FF2) as c:
                    hidden(l, c, False)
                with dve.Fori(0, FF2 // 2) as c:
                    split_lo(N_DOWN[l] + 2, c)
                    split_lo(N_DOWN[l] + 3, c)
                v = V_FFN[l]
                for m in range(KT):
                    add_delta(v, m, m)
                    if m:
                        gained_lo(v, m - 1, xp_hi, xp_lo)
                gained_lo(v, KT - 1, xp_hi, xp_lo)
                for j in range(2):
                    dve.wait_ge(pt_hi_done[l], j + 1)
                    dve.tensor_tensor(pt_lo[:, j, :], ps[:, j, :], pt_hi[:, j, :].bitcast(F32), ALU.subtract).then_inc(pt_lo_done[l], 1)
                split_lo(N_PLE[l] + 1)
                factor(v)
                split_lo(N_PLE[l] + 2)
                dve.wait_ge(r_bc_done, spreads(v))
                v = V_PLE[l]

                def add_embedding(m):
                    dve.wait_ge(d_done[l], m + 1)
                    dve.tensor_tensor(h[:, m, :], h[:, m, :], ple_t[:, m % 2, :], ALU.add).then_inc(h_done, 1)

                for m in range(KT):
                    dve.wait_ge(pg_ready[l], m + 1)
                    if m >= 2:
                        dve.wait_ge(h_done, KT * v + m - 1)
                    dve.tensor_tensor(ple_t[:, m % 2, :], ps[:, 4 + m % 2, :], r_tok[:, :], ALU.mult).then_inc(pg_done[l], 1)
                    if m:
                        add_embedding(m - 1)
                    if m % 2 and N_PLE[l] + 3 + m // 2 < N_ALL:
                        split_lo(N_PLE[l] + 3 + m // 2)
                    if m >= 2 and l == 0:
                        gained_lo(3, m - 2, x_hi, x_lo)
                add_embedding(KT - 1)
                if l == 0:
                    gained_lo(3, KT - 2, x_hi, x_lo)
                    gained_lo(3, KT - 1, x_hi, x_lo)

            dve.wait_ge(ssq_ready, 6)
            mean(6, ps[:, 7, 0:TB])
            dve.wait_ge(r_done, 7)
            dve.wait_ge(gain_in, 16)
            for j in range(2 * TB):
                half, t = divmod(j, TB)
                dve.wait_ge(fin_ready, j + 1)
                dve.scalar_tensor_tensor(out=result[:, j, :], in0=ps[:, j % 7, :], scalar=r_col[:, 24 + t:25 + t],
                                         in1=gain_final[:, half * 512:(half + 1) * 512], op0=ALU.mult, op1=ALU.mult).then_inc(fin_done, 1)

        @block.tensor
        def _(pe):
            def weights(n, it=0):
                pe.wait_ge(w_lo_done, n + 1 + 2 * it)

            def split_product(outp, slot, cols_of, hi, lo, kts, ready=None, first=True, last=True):
                for a, kt in enumerate(kts):
                    if ready is not None:
                        pe.wait_ge(*ready(kt))
                    c0 = cols_of(kt)
                    wh, wl = w_hi[:, slot, c0:c0 + P], w_lo[:, slot, c0:c0 + P]
                    pe.matmul(outp, wh, hi(kt), start=first and a == 0, stop=False)
                    pe.matmul(outp, wl, hi(kt), start=False, stop=False)
                    ins = pe.matmul(outp, wh, lo(kt), start=False, stop=last and a == len(kts) - 1)
                return ins

            def split_product_nat(outp, slot, t, ready=None):
                for kt in range(KT):
                    if ready is not None:
                        pe.wait_ge(*ready(kt))
                    c0 = kt * CW
                    wh, wl = w_hi[:, slot, c0:c0 + CW], w_lo[:, slot, c0:c0 + CW]
                    xh, xl = x_hi[:, kt, t * P:(t + 1) * P], x_lo[:, kt, t * P:(t + 1) * P]
                    pe.matmul(outp, xh, wh, start=kt == 0, stop=False)
                    pe.matmul(outp, xh, wl, start=False, stop=False)
                    ins = pe.matmul(outp, xl, wh, start=False, stop=kt == KT - 1)
                return ins

            def xh(kt):
                return x_hi[:, kt, :]

            def xl(kt):
                return x_lo[:, kt, :]

            def square_sums(v):
                pe.wait_ge(sq_sum_done, (KT - 1) * v)
                for t in range(TB):
                    ins = pe.matmul(ps[:, 7, t:t + 1], sq_sum[:, t * P:(t + 1) * P], ones[:, 0:1], start=True, stop=True)
                ins.then_inc(ssq_ready, 1)

            def spread_factor(v):
                pe.wait_ge(diag_done, spreads(v))
                pe.matmul(ps[:, 6, :], ones[:, :], diag[:, :, :].rearrange("q t n -> q (t n)"), start=True, stop=True).then_inc(r_bc_ready, 1)

            pe.wait_ge(consts, 17)
            pe.wait_ge(gains_in, 48)
            pe.transpose(ps[:, 0, 0:P], gains_nat[:, :], ident[:, :]).then_inc(gains_t_ready, 1)
            for t in range(TB):
                pe.wait_ge(x_in[t], 16)
            for kt in range(KT):
                if kt >= 4:
                    pe.wait_ge(h_done, kt - 3)
                for t in range(TB):
                    ins = pe.transpose(ps[:, 2 + kt % 4, t * P:(t + 1) * P], x_nat[:, t, kt * P:(kt + 1) * P], ident[:, :])
                ins.then_inc(xt_ready, 1)
            spread_factor(0)

            def project_qk(g, j):
                n = GROUP_CHUNK[g] + (0 if j < 2 else 2)
                weights(n)
                if 4 * g + j:
                    pe.wait_ge(qk_done, 4 * g + j)
                if g:
                    pe.wait_ge(v_done, 4 * g + j)
                ready = (lambda kt: (x_lo_done, kt + 1)) if 4 * g + j == 0 else None
                split_product(ps[:, 0, :], n % 2, lambda kt: kt * CW + (j % 2) * P, xh, xl, range(KT), ready).then_inc(qk_ready, 1)

            def project_v(g, t):
                n = GROUP_CHUNK[g] + 1
                weights(n)
                if 4 * g + t:
                    pe.wait_ge(v_done, 4 * g + t)
                if g:
                    pe.wait_ge(qk_done, 4 * g + t + 1)
                split_product_nat(ps[:, 0 if g else 1, 0:CW], n % 2, t).then_inc(v_ready, 1)

            for i in range(4):
                project_qk(0, i)
                project_v(0, i)
            weights(GATE_CHUNK)
            split_product(ps[:, 7, :], GATE_CHUNK % 2, lambda kt: kt * P, xh, xl, range(KT)).then_inc(gate_ready, 1)

            def part(region, b, c0, width):
                return region[:, OFF[b] + c0:OFF[b] + c0 + width]

            def scores0(s):
                g, i = divmod(s, 4)
                slot, half = (2 * g + i // 2) % 4, i % 2
                pe.wait_ge(qk_done, 4 * g + 4)
                if s == 1:
                    pe.wait_ge(gate_step, 1)
                if s >= 2:
                    pe.wait_ge(wt_done, s - 1)
                for b in (0, 1, 3, 2):
                    q = TB - 1 - b
                    keys = k_pad[:, slot, half, b * P:(b + 1) * P] if g < 2 else k_pad[:, slot, half, 0:LEN[b]]
                    queries = q_pair[:, slot, b * P:SEQ] if g < 2 else q_pair[:, slot, q * P:(q + 1) * P]
                    lhs, rhs = (keys, queries) if g < 2 else (queries, keys)
                    pe.matmul(part(z[s % 2], b, 0, LEN[b]), lhs, rhs, start=b != 3, stop=False, skip_group_check=True)
                    ins = pe.matmul(part(z[s % 2], b, 0 if g < 2 else q * P, P), ident_b[:, :], (mask_kq if g < 2 else mask_qk)[:, :],
                                    start=False, stop=g >= 2, skip_group_check=True)
                ins.then_inc(z_ready, 1)

            def sums0(s):
                pe.wait_ge(sb_l, s + 1)
                for b in range(TB):
                    for j in range(b, TB):
                        ins = pe.matmul(part(z[s % 2], b, (j - b) * P, LEN[j]), (neg_tri if j == b else neg_ones)[:, :],
                                        part(B[2], j, 0, LEN[j]), start=False, stop=j == TB - 1, skip_group_check=True)
                ins.then_inc(c_ready, 1)

            def turn0(s):
                pe.wait_ge(fx_norm, s - 7)
                for b in range(TB):
                    for q in range(b, TB):
                        ins = pe.transpose(part(z[s % 2], b, (q - b) * P, P), part(B[s % 2], TB - 1 - q, b * P, P), ident[:, :])
                ins.then_inc(fx_t_ready, 1)

            def output0(s):
                g, i = divmod(s, 4)
                pe.wait_ge(wt_done, s + 1)
                pe.wait_ge(v_done, 4 * g + 4)
                if s:
                    pe.wait_ge(o_lo_done, s)
                for b in range(TB):
                    ins = pe.matmul(ps[:, 1, b * P:SEQ], v_nat[:, g % 2, b, (i // 2) * P:(i // 2 + 1) * P], part(B[3 + s % 2], b, 0, LEN[b]),
                                    start=b == 0, stop=b == TB - 1, skip_group_check=True)
                ins.then_inc(pv_ready, 1)

            scores0(0)
            for s in range(NHEADS):
                g, i = divmod(s, 4)
                middle = sums0 if g < 2 else turn0
                if g == 3 or i < 3:
                    if s + 1 < NHEADS:
                        scores0(s + 1)
                    if g < 3:
                        project_qk(g + 1, i)
                    middle(s)
                else:
                    project_qk(g + 1, i)
                    middle(s)
                    scores0(s + 1)
                if g < 3:
                    project_v(g + 1, i)
                if s:
                    output0(s - 1)
            output0(NHEADS - 1)

            for l in L:
                if l == 1:
                    def project(idx):
                        c, t = divmod(idx, 4)
                        weights(N_IN1 + c)
                        if idx >= 2:
                            prev = idx - 2 if idx < 15 else idx - 1
                            if 4 <= prev < 8:
                                pe.wait_ge(v1_done, prev - 3)
                            else:
                                pe.wait_ge(rope_step, (prev if prev < 4 else prev - 4) + 1)
                            if prev >= 8:
                                pe.wait_ge(tr_done, prev - 3)
                        ready = (lambda kt: (x_lo_done, 3 * KT + kt + 1)) if idx == 0 else None
                        split_product_nat(ps[:, bank1(idx), 0:CW], (N_IN1 + c) % 2, t, ready).then_inc(in_ready, 1)

                    def turn(idx):
                        if idx < 4:
                            pe.wait_ge(rope_done, idx + 1)
                            if idx:
                                pe.wait_ge(tr_done, idx)
                            for g in range(NKV):
                                ins = pe.transpose(ps[:, 6, g * P:(g + 1) * P], rope_k[:, g, :, :].rearrange("q d n -> q (d n)"), ident[:, :])
                        else:
                            pe.wait_ge(rope_done, idx - 3)
                            for j in range(2):
                                ins = pe.transpose(ps[:, bank1(idx), CW + j * P:CW + (j + 1) * P], rope_q[:, j * P:(j + 1) * P], ident[:, :])
                        ins.then_inc(tr_ready, 1)

                    def scores(s):
                        g, half, b0 = s // 4, s % 2, 2 + 2 * (s % 2)
                        pe.wait_ge(tr_done, 4 + 4 * g + 4)
                        if s >= 2:
                            pe.wait_ge(s_exp, 5 * (s - 1))
                        for b in range(TB):
                            dst = ps[:, b0 + b // 2, :]
                            if b % 2 == 0:
                                mask = mask_win0 if b == 0 else mask_win
                                pe.matmul(dst, ident_b[:, :], mask[:, :, :].rearrange("q a n -> q (a n)"), start=True, stop=False, skip_group_check=True)
                            k0 = max(b - 1, 0)
                            c0 = (b % 2) * 256 + (P if b == 0 else 0)
                            width = (b - k0 + 1) * P
                            ins = pe.matmul(dst[:, c0:c0 + width], q1_pair[:, s // 2, b * P:(b + 1) * P],
                                            k1_pad[:, g, half, k0 * P:(b + 1) * P], start=False, stop=True, skip_group_check=True)
                        ins.then_inc(s_ready, 1)

                    for idx in range(13):
                        project(idx)
                        prev = idx - 1
                        if idx == 0:
                            square_sums(3)
                        if 0 <= prev and not 4 <= prev < 8:
                            turn(prev)

                    def turn_weights(s):
                        pe.wait_ge(s_norm, s + 1)
                        if s:
                            pe.wait_ge(t1_done, s)
                        for b in range(TB):
                            for j in range(min(2, TB - b)):
                                c0 = (2 * b + j) * P
                                ins = pe.transpose(ps_flat[:, 6 * 512 + c0:6 * 512 + c0 + P], p1[:, s % 2, b + j, (1 - j) * P:(2 - j) * P], ident[:, :])
                        ins.then_inc(t1_ready, 1)

                    def output(s):
                        pe.wait_ge(t1_done, s + 1)
                        pe.wait_ge(v1_done, 4)
                        if s:
                            pe.wait_ge(o1_lo_done, s)
                        else:
                            pe.wait_ge(tr_done, 10)
                        for b in range(TB):
                            width = min(2, TB - b) * P
                            ins = pe.matmul(ps[:, 1, b * P:b * P + width], v1_dup[:, b, s // 4, :, :].rearrange("q d n -> q (d n)"),
                                            p1_t[:, s % 2, 2 * b * P:2 * b * P + width], start=b == 0, stop=b == TB - 1, skip_group_check=True)
                        ins.then_inc(pv1_ready, 1)

                    scores(0)
                    project(13)
                    turn(12)
                    scores(1)
                    project(14)
                    turn(13)
                    for s in range(NQ):
                        turn_weights(s)
                        if s + 2 < NQ:
                            scores(s + 2)
                        if s < 10:
                            turn(14 + s)
                        output(s)
                        if s < 9:
                            project(15 + s)

                v = V_MIX[l]
                order = [4, 5, 6, 7, 0, 1, 2, 3] if l == 0 else list(range(KT))
                o_ready = o_lo_done if l == 0 else o1_lo_done
                for m in range(KT):
                    n = N_OUT[l] + m // 2
                    weights(n)
                    if m >= 2:
                        pe.wait_ge(h_done, KT * v + m - 1)
                    ready = (lambda kt: (o_ready, 2 * order.index(kt) + 2)) if m == 0 else None
                    split_product(ps[:, 4 + m % 2, :], n % 2, lambda kt: kt * CW + (m % 2) * P, lambda kt: o_hi[:, kt, :],
                                  lambda kt: o_lo[:, kt, :], order, ready).then_inc(delta_ready, 1)

                def hidden(c, first):
                    for j in range(2):
                        weights(N_FFN[l], c)
                        if not first:
                            pe.wait_ge(g_done[l], c * 2 + j - 1)
                        ready = (lambda kt: (x_lo_done, KT * v + kt + 1)) if first and j == 0 else None
                        split_product(ps[:, j, :], N_FFN[l] % 2, lambda kt: kt * CW + j * P, xh, xl, range(KT), ready).then_inc(g_ready[l], 1)
                        if first and j == 0:
                            square_sums(v)
                        if first and j == 1:
                            spread_factor(v)
                    for j in range(2):
                        weights(N_FFN[l] + 1, c)
                        if not first:
                            pe.wait_ge(u_done[l], c * 2 + j - 1)
                        split_product(ps[:, 2 + j, :], (N_FFN[l] + 1) % 2, lambda kt: kt * CW + j * P, xh, xl, range(KT)).then_inc(u_ready[l], 1)

                hidden(0, True)
                with pe.Fori(1, FF2) as c:
                    hidden(c, False)

                def down(n, it, tiles, first):
                    weights(n, it)
                    d = n - N_DOWN[l]
                    pe.wait_ge(a_lo_done[l], 2 * d + 2 + it * 4)
                    for a, m in enumerate(tiles):
                        for j in range(2):
                            k0 = (2 * d + j) * SEQ + it * (4 * SEQ)
                            wh = w_hi[:, n % 2, j * DM + m * P:j * DM + (m + 1) * P]
                            wl = w_lo[:, n % 2, j * DM + m * P:j * DM + (m + 1) * P]
                            ah = act_hi[:, bass.ds(k0, SEQ)]
                            al = act_lo[:, bass.ds(k0, SEQ)]
                            if first and a == 4 and j == 0:
                                pe.wait_ge(u_done[l], FT)
                            last = d == FF2 - 1 and j == 1
                            pe.matmul(ps[:, m, :], wh, ah, start=first and j == 0, stop=False, skip_group_check=True)
                            pe.matmul(ps[:, m, :], wl, ah, start=False, stop=False, skip_group_check=True)
                            ins = pe.matmul(ps[:, m, :], wh, al, start=False, stop=last, skip_group_check=True)
                        if d == FF2 - 1:
                            ins.then_inc(delta_ready, 1)
                    if d < FF2 - 1:
                        ins.then_inc(down_used[l], 1)

                down(N_DOWN[l], 0, [4, 5, 6, 7, 0, 1, 2, 3], True)
                down(N_DOWN[l] + 1, 0, range(KT), False)
                with pe.Fori(1, FF2 // 2) as c:
                    down(N_DOWN[l], c, range(KT), False)
                    down(N_DOWN[l] + 1, c, range(KT), False)
                down(N_DOWN[l] + FF2 - 1, 0, range(KT), False)

                v = V_FFN[l]
                pe.wait_ge(p_in[l], 16)
                for j in range(2):
                    pe.wait_ge(h_done, KT * v + j + 1)
                    for t in range(TB):
                        ins = pe.transpose(ps[:, j, t * P:(t + 1) * P], p_nat[:, t, j * P:(j + 1) * P], ident[:, :])
                    ins.then_inc(pt_ready[l], 1)
                n = N_PLE[l]
                weights(n)
                pe.wait_ge(pt_lo_done[l], 2)
                for m in range(KT):
                    if m < 2:
                        pe.wait_ge(h_done, KT * v + 3 + m)
                    else:
                        pe.wait_ge(e_done[l], m - 1)
                    split_product(ps[:, 2 + m % 2, :], n % 2, lambda kt: kt * DM + m * P, lambda kt: pt_hi[:, kt, :],
                                  lambda kt: pt_lo[:, kt, :], range(2)).then_inc(e_ready[l], 1)
                pe.wait_ge(h_done, KT * v + KT)
                square_sums(v)
                for m in range(KT):
                    n = N_PLE[l] + 1 + m // 2
                    weights(n)
                    if m >= 2:
                        pe.wait_ge(pg_done[l], m - 1)
                    ready = (lambda kt: (x_lo_done, KT * v + kt + 1)) if m == 0 else None
                    split_product(ps[:, 4 + m % 2, :], n % 2, lambda kt: kt * CW + (m % 2) * P, lambda kt: xp_hi[:, kt, :],
                                  lambda kt: xp_lo[:, kt, :], range(KT), ready).then_inc(pg_ready[l], 1)
                    if m == 0:
                        spread_factor(v)

            for half in range(2):
                for kt in range(4 * half, 4 * half + 4):
                    pe.wait_ge(h_done, KT * 6 + kt + 1)
                if half:
                    square_sums(6)
                for t in range(TB):
                    j = half * TB + t
                    if j == 4:
                        pe.wait_ge(pg_done[1], KT)
                    if j == 7:
                        pe.wait_ge(fin_done, 1)
                    for a in range(4):
                        ins = pe.transpose(ps[:, j % 7, a * P:(a + 1) * P], h[:, 4 * half + a, t * P:(t + 1) * P], ident[:, :])
                    ins.then_inc(fin_ready, 1)


_INS = ["x", "p", "positions", "norm_mix", "norm_ffn", "norm_ple", "norm_final", "ev_w_in", "ev_b_f", "ev_w_out",
        "od_w_in", "od_sinks", "od_w_out", "ffn_w_gate", "ffn_w_up", "ffn_w_down", "ple_w_proj", "ple_w_gate"]


def kernel(**inputs):
    import numpy as _np
    import concourse.bacc as _bacc
    from concourse import mybir as _mybir
    from concourse.bass_utils import run_bass_kernel_spmd as _run

    nc = _bacc.Bacc("TRN2", target_bir_lowering=False, num_devices=1, dynamic_dma_scratch_size=4096)
    arrays, args = {}, []
    for name in _INS:
        a = _np.ascontiguousarray(inputs[name])
        arrays[f"in_{name}"] = a
        args.append(nc.dram_tensor(f"in_{name}", a.shape, _mybir.dt.from_np(a.dtype), kind="ExternalInput").ap())
    shape = arrays["in_x"].shape
    args.append(nc.dram_tensor("out_0", shape, _mybir.dt.from_np(_np.dtype("float32")), kind="ExternalOutput").ap())
    hybrid_trunk(nc, *args)
    r = _run(nc, [arrays], core_ids=[0])
    return r.results[0]["out_0"]
```

```python
import math
from contextlib import ExitStack

import numpy as np

import concourse.bass as bass
from concourse import mybir

F32 = mybir.dt.float32
F32R = mybir.dt.float32r
BF16 = mybir.dt.bfloat16
I32 = mybir.dt.int32
ACT = mybir.ActivationFunctionType
ALU = mybir.AluOpType
AX_X = mybir.AxisListType.X

P = 128
NEG = -1e30
EPS = 1e-6
THETA = 10000.0
LOWEST = -3.0e38


def hybrid_trunk(nc, x, p, positions, norm_mix, norm_ffn, norm_ple, norm_final, ev_w_in, ev_b_f, ev_w_out,
                 od_w_in, od_sinks, od_w_out, ffn_w_gate, ffn_w_up, ffn_w_down, ple_w_proj, ple_w_gate, out):
    _, SEQ, DM = x.shape
    DEPTH = p.shape[0]
    PLE = p.shape[3]
    DFF = ffn_w_gate.shape[2]
    HD = 64
    HALF = HD // 2
    NFOX = ev_b_f.shape[1]
    NHEADS = DM // HD
    FOXW = NFOX * HD
    SBW = DM - FOXW
    NQ = od_sinks.shape[1]
    NKV = (od_w_in.shape[2] - NQ * HD) // (2 * HD)
    SCALE = HD ** -0.5
    KT = DM // P
    TB = SEQ // P
    CW = 256
    CHUNK = KT * CW
    FF2 = DFF // CW
    FT = DFF // P
    assert (SEQ, DM, DEPTH, PLE, DFF, NFOX, NQ, NKV) == (512, 1024, 2, 256, 2816, 8, 16, 4)

    KB = 1024
    base = (nc.sbuf_base + 63) // 64 * 64

    def at(name, shape, dt, kb):
        return nc.alloc_sbuf_tensor_at(name, shape, dt, offset=base + int(kb * KB))

    h = at("h", [P, KT, SEQ], F32, 0)
    x_hi = at("x_hi", [P, KT, SEQ], F32R, 16)
    x_lo = at("x_lo", [P, KT, SEQ], F32R, 32)
    emb = at("emb", [P, KT, SEQ], F32, 32)
    w_raw = at("w_raw", [P, 2, CHUNK], F32, 48)
    w_hi = at("w_hi", [P, 2, CHUNK], F32R, 64)
    w_lo = at("w_lo", [P, 2, CHUNK], F32R, 80)
    X = 96
    act_hi = at("act_hi", [P, FT * SEQ], F32R, X)
    act_lo = at("act_lo", [P, FT * SEQ], F32R, X + 44)
    o_hi = at("o_hi", [P, KT, SEQ], F32R, X)
    o_lo = at("o_lo", [P, KT, SEQ], F32R, X + 16)
    l_hi = at("l_hi", [P, 1280], F32R, X)
    l_lo = at("l_lo", [P, 1280], F32R, X + 16)
    v_nat = at("v_nat", [P, 2, TB, CW], F32, X + 32)
    gate_f = at("gate_f", [NFOX, SEQ], F32, X + 40)
    gate_t = at("gate_t", [NFOX, SEQ], F32, X + 42)
    gate_cum = at("gate_cum", [NFOX, SEQ], F32, X + 44)
    gate_zero = at("gate_zero", [NFOX, SEQ], F32, X + 46)
    q_pair = at("q_pair", [P, 4, SEQ], F32, X + 48)
    k_pad = at("k_pad", [P, 4, 2, SEQ], F32, X + 56)
    x_nat = at("x_nat", [P, TB, DM], F32, X + 72)
    f_keys = at("f_keys", [P, NFOX, SEQ], F32, X + 72)
    q1_parts = at("q1_parts", [P, NQ // 2, 2, SEQ], F32R, X + 32)
    k1_hi = at("k1_hi", [P, NKV, SEQ], F32R, X + 64)
    k1_lo = at("k1_lo", [P, NKV, SEQ], F32R, X + 72)
    v1_dup = at("v1_dup", [P, TB, NKV, 2, HD], F32, X + 80)
    xp_hi = at("xp_hi", [P, KT, SEQ], F32R, X)
    xp_lo = at("xp_lo", [P, KT, SEQ], F32R, X + 16)
    gain_final = at("gain_final", [P, DM], F32, X + 76)
    result = at("result", [P, 2 * TB, SEQ], F32, X)
    C = 184
    ident = at("ident", [P, P], F32, C)
    neg_tri = at("neg_tri", [P, P], F32R, C + 0.5)
    neg_ones = at("neg_ones", [P, P], F32R, C + 1)
    ones = at("ones", [P, P], F32, C + 1.5)
    ident_b = at("ident_b", [P, P], BF16, C + 2)
    mask_qk = at("mask_qk", [P, P], BF16, C + 2.25)
    mask_kq = at("mask_kq", [P, P], BF16, C + 2.5)
    mask_win = at("mask_win", [P, 4, P], BF16, C + 2.75)
    mask_win0 = at("mask_win0", [P, 4, P], BF16, C + 3.75)
    r_tok = at("r_tok", [P, SEQ], F32, C + 4.75)
    cos_t = at("cos_t", [P, TB, 2, HALF], F32, C + 6.75)
    sin_t = at("sin_t", [P, TB, 2, HALF], F32, C + 7.75)
    gain_t = at("gain_t", [P, P], F32, C + 8.75)
    inv_freq = at("inv_freq", [P, HALF], F32, C + 9.25)
    small = at("small", [P, 160], F32, C + 9.375)
    pos_i = at("pos_i", [P, TB], I32, C + 10)
    minus_half = small[:, 0:4]
    r_col = small[:, 4:32]
    mean_sq = small[:, 32:36]
    ssq0 = small[:, 36:40]
    gate_bias = small[0:NFOX, 40:41]
    sinks = small[:, 44:60]
    sinks8 = small[:, 60:76]
    row_max = small[:, 76:84]
    neg_max = small[:, 84:92]
    row_sum = small[:, 92:100]
    row_inv = small[:, 100:108]
    sink_exp = small[:, 108:116]
    den = small[:, 116:124]
    pos_f = small[:, 124:128]
    W = 194.125
    B = [at(f"score_{i}", [P, 1280], F32, W + 5 * i) for i in range(5)]
    gains_nat = at("gains_nat", [P, P], F32, W)
    neg_tri_f = at("neg_tri_f", [P, P], F32, W + 5)
    neg_ones_f = at("neg_ones_f", [P, P], F32, W + 5.5)
    diag = at("diag", [P, TB, P], F32, W + 22)
    gs = at("gs", [P, 2, SEQ], F32, W)
    up = at("up", [P, 2, SEQ], F32, W + 4)
    sq = at("sq", [P, 2, SEQ], F32, W + 8)
    sq_sum = at("sq_sum", [P, SEQ], F32, W + 12)
    ple_t = at("ple_t", [P, 2, SEQ], F32, W + 14)
    p_nat = at("p_nat", [P, TB, PLE], F32, W + 14)
    pt_hi = at("pt_hi", [P, 2, SEQ], F32R, W + 14)
    pt_lo = at("pt_lo", [P, 2, SEQ], F32R, W + 18)
    x_sq = at("x_sq", [P, DM], F32, W + 10)
    ang = at("ang", [P, 2, TB, HALF], F32, W + 18)
    turns_i = at("turns_i", [P, 2, TB, HALF], I32, W + 19)
    turns = at("turns", [P, 2, TB, HALF], F32, W + 20)
    trig = at("trig", [P, 2, TB, HALF], F32, W + 21)
    rope_a = at("rope_a", [P, CW], F32, W)
    rope_b = at("rope_b", [P, CW], F32, W + 1)
    rope_q = at("rope_q", [P, CW], F32, W + 2)
    rope_k = at("rope_k", [P, NKV, 2, HD], F32, W + 3)
    p1_t = at("p1_t", [P, 2, 7 * P], F32, W + 5)
    p1 = at("p1", [P, 2, TB, 2 * P], F32, W + 14)

    f_dram = nc.dram_tensor("forget_cumsum", (NFOX, SEQ), F32).ap()

    OFF = [0, 512, 1024, 896]
    LEN = [(TB - b) * P for b in range(TB)]

    def cols(w, c0):
        return w.rearrange("(k q) n -> q k n", q=P)[:, :, c0:c0 + CW]

    def rows(w, k0):
        return w.rearrange("(k q) n -> q k n", q=P)[:, k0:k0 + 2, :]

    w_in0, w_in1 = ev_w_in[0], od_w_in[0]
    SB0 = 3 * FOXW
    GROUPS = [(SB0 + CW * g, SB0 + 2 * SBW + CW * g, SB0 + SBW + CW * g) for g in range(2)]
    GROUPS += [(CW * g, 2 * FOXW + CW * g, FOXW + CW * g) for g in range(2)]
    GROUP_CHUNK = [0, 4, 7, 10]
    GATE_CHUNK = 3
    N_OUT = [13, 61]
    N_FFN = [17, 65]
    N_EMB = [n + 2 * FF2 for n in N_FFN]
    N_DOWN = [n + 1 for n in N_EMB]
    N_GATE = [n + FF2 for n in N_DOWN]
    N_IN1 = N_GATE[0] + 4
    N_ALL = N_GATE[1] + 4
    assert N_IN1 == 55 and N_IN1 + 6 == N_OUT[1] and N_ALL == 103

    with ExitStack() as ctx:
        def sem(name):
            return ctx.enter_context(nc.semaphore(name))

        ps = ctx.enter_context(nc.psum_tensor("ps", [P, 8, 512], F32))
        ps_flat = ps[:, :, :].rearrange("q b n -> q (b n)")
        z = [ps_flat[:, (2 + 3 * k) * 512:(2 + 3 * k) * 512 + 1280] for k in range(2)]

        x_in = [sem(f"x_in_{t}") for t in range(TB)]
        gains_in, small_in = sem("gains_in"), [sem(f"small_in_{i}") for i in range(3)]
        slot_in = [sem(f"slot_in_{i}") for i in range(2)]
        gate_cols_in = sem("gate_cols_in")
        p_in, gain_in = [sem(f"p_in_{i}") for i in range(2)], sem("gain_in")
        f_out, f_in = sem("f_out"), sem("f_in")
        out_sem = sem("out_sem")
        consts = sem("consts")
        k_zeroed = sem("k_zeroed")
        w_hi_done, w_lo_done = sem("w_hi_done"), sem("w_lo_done")
        h_done, x_hi_done, x_lo_done = sem("h_done"), sem("x_hi_done"), sem("x_lo_done")
        xt_ready = sem("xt_ready")
        gains_t_ready, gains_t_done = sem("gains_t_ready"), sem("gains_t_done")
        delta_ready = sem("delta_ready")
        sq_done, sq_sum_done, x_sq_done = sem("sq_done"), sem("sq_sum_done"), sem("x_sq_done")
        ssq_ready, mean_done, r_done = sem("ssq_ready"), sem("mean_done"), sem("r_done")
        diag_done, r_bc_ready, r_bc_done = sem("diag_done"), sem("r_bc_ready"), sem("r_bc_done")
        qk_ready, qk_done, v_ready, v_done = sem("qk_ready"), sem("qk_done"), sem("v_ready"), sem("v_done")
        gate_ready, gate_step = sem("gate_ready"), sem("gate_step")
        gate_abs = sem("gate_abs")
        z_ready, sb_abs, sb_l, c_ready = sem("z_ready"), sem("sb_abs"), sem("sb_l"), sem("c_ready")
        neg_done, l_hi_done, l_lo_done = sem("neg_done"), sem("l_hi_done"), sem("l_lo_done")
        fx_max, fx_neg, fx_exp, fx_inv, fx_norm = (sem(n) for n in ("fx_max", "fx_neg", "fx_exp", "fx_inv", "fx_norm"))
        fx_t_ready, wt_done = sem("fx_t_ready"), sem("wt_done")
        pv_ready, o_hi_done, o_lo_done = sem("pv_ready"), sem("o_hi_done"), sem("o_lo_done")
        trig_step, trig_done, rope_angle = sem("trig_step"), sem("trig_done"), sem("rope_angle")
        in_ready, rope_step, rope_done, v1_done = sem("in_ready"), sem("rope_step"), sem("rope_done"), sem("v1_done")
        tr_ready, tr_hi_done, tr_done, table_step = (sem(n) for n in ("tr_ready", "tr_hi_done", "tr_done", "table_step"))
        s_ready, s_max, s_neg, s_exp, s_den, s_inv, s_norm = (
            sem(n) for n in ("s_ready", "s_max", "s_neg", "s_exp", "s_den", "s_inv", "s_norm"))
        t1_ready, t1_done, pv1_ready, o1_hi_done, o1_lo_done = (
            sem(n) for n in ("t1_ready", "t1_done", "pv1_ready", "o1_hi_done", "o1_lo_done"))
        L = range(DEPTH)
        g_ready, u_ready, g_done, u_done = ([sem(f"{n}_{i}") for i in L] for n in ("g_ready", "u_ready", "g_done", "u_done"))
        silu_done, a_done, a_hi_done, a_lo_done = (
            [sem(f"{n}_{i}") for i in L] for n in ("silu_done", "a_done", "a_hi_done", "a_lo_done"))
        down_used = [sem(f"down_used_{i}") for i in L]
        pt_ready, pt_hi_done, pt_lo_done = ([sem(f"{n}_{i}") for i in L] for n in ("pt_ready", "pt_hi_done", "pt_lo_done"))
        e_ready, e_done, pg_ready, pg_done = ([sem(f"{n}_{i}") for i in L] for n in ("e_ready", "e_done", "pg_ready", "pg_done"))
        sig_done, d_done = ([sem(f"{n}_{i}") for i in L] for n in ("sig_done", "d_done"))
        fin_ready, fin_done, fin_even, fin_odd = sem("fin_ready"), sem("fin_done"), sem("fin_even"), sem("fin_odd")

        V_MIX, V_FFN, V_PLE = [1, 4], [2, 5], [3, 6]
        DELTA = {1: 0, 2: 8, 4: 16, 5: 24}

        def bank1(idx):
            return idx if idx < 6 else idx % 2 if idx < 15 else 0

        def turn_bank(idx):
            return 6 + idx % 2 if idx < 14 else 0

        def e_bank(m):
            return 4 + (m + 2) % 4

        def fin_bank(j):
            return (4 + j) % 7

        def out_bank(m):
            return 4 + (m + 1) % 2 if m else 0

        def spreads(v):
            return v + 1 if v < 3 else v

        def last_product(n):
            for g, n0 in enumerate(GROUP_CHUNK):
                if n == n0:
                    return qk_ready, 4 * g + 2
                if n == n0 + 1:
                    return v_ready, 4 * g + 4
                if n == n0 + 2:
                    return qk_ready, 4 * g + 4
            if n == GATE_CHUNK:
                return gate_ready, 1
            for i in L:
                if N_OUT[i] <= n < N_OUT[i] + 4:
                    return delta_ready, DELTA[V_MIX[i]] + 2 * (n - N_OUT[i]) + 2
                if N_FFN[i] <= n < N_EMB[i]:
                    c, u = divmod(n - N_FFN[i], 2)
                    return (u_ready if u else g_ready)[i], 2 * c + 2
                if N_DOWN[i] <= n < N_DOWN[i] + FF2 - 1:
                    return down_used[i], n - N_DOWN[i] + 1
                if n == N_DOWN[i] + FF2 - 1:
                    return delta_ready, DELTA[V_FFN[i]] + KT
                if n == N_EMB[i]:
                    return e_ready[i], KT
                if N_GATE[i] <= n < N_GATE[i] + 4:
                    return pg_ready[i], 2 * (n - N_GATE[i]) + 2
            return in_ready, 4 * (n - N_IN1) + 4

        block = ctx.enter_context(nc.Block())

        @block.sync
        def _(sp):
            def load(n, src, it=0):
                if n >= 2:
                    sp.wait_ge(w_lo_done, n - 1 + 2 * it)
                k = src.shape[1]
                dst = w_raw[:, n % 2, :].rearrange("q (k n) -> q k n", k=k)
                sp.dma_start(dst, src).then_inc(slot_in[n % 2], 16)

            for t in range(TB):
                sp.dma_start(x_nat[:, t, :], x[0, t * P:(t + 1) * P, :]).then_inc(x_in[t], 16)
            for g, (q0, v0, k0) in enumerate(GROUPS):
                n = GROUP_CHUNK[g]
                load(n, cols(w_in0, q0))
                load(n + 1, cols(w_in0, v0))
                load(n + 2, cols(w_in0, k0))
                if g == 0:
                    sp.wait_ge(w_lo_done, GATE_CHUNK - 1)
                    dst = w_raw[:, GATE_CHUNK % 2, 0:KT * P].rearrange("q (k n) -> q k n", k=KT)
                    src = w_in0.rearrange("(k q) n -> q k n", q=P)
                    sp.dma_start(dst[:, :, NFOX:P], src[:, :, 0:P - NFOX]).then_inc(slot_in[GATE_CHUNK % 2], 16)
                    sp.dma_start(dst[:, :, 0:NFOX], src[:, :, SB0 + 3 * SBW:SB0 + 3 * SBW + NFOX]).then_inc(gate_cols_in, 16)
                if g == 1:
                    sp.wait_ge(gate_step, 4)
                    sp.dma_start(f_dram, gate_cum[:, :]).then_inc(f_out, 16)
                    sp.wait_ge(h_done, KT)
                    sp.wait_ge(x_sq_done, TB)
                    sp.wait_ge(f_out, 16)
                    for f in range(NFOX):
                        sp.dma_start(f_keys[:, f, :], f_dram[f:f + 1, :].broadcast_to([P, SEQ])).then_inc(f_in, 16)
            for i in L:
                if i == 1:
                    kv0 = NQ * HD
                    for c, c0 in enumerate([kv0, kv0 + CW] + [CW * j for j in range(4)]):
                        load(N_IN1 + c, cols(w_in1, c0))
                w_out = (ev_w_out, od_w_out)[i][0]
                for c in range(4):
                    load(N_OUT[i] + c, cols(w_out, CW * c))
                gate_v = ffn_w_gate[i].rearrange("(k q) n -> q k n", q=P)
                up_v = ffn_w_up[i].rearrange("(k q) n -> q k n", q=P)
                with sp.Fori(0, FF2) as c:
                    load(N_FFN[i], gate_v[:, :, bass.ds(c * CW, CW)], c)
                    load(N_FFN[i] + 1, up_v[:, :, bass.ds(c * CW, CW)], c)
                if i == 0:
                    sp.wait_ge(table_step, 1)
                else:
                    sp.wait_ge(h_done, KT * V_MIX[1] + 1)
                sp.dma_start(p_nat[:, :, :], p[i, 0].rearrange("(t q) n -> q t n", q=P)).then_inc(p_in[i], 16)
                load(N_EMB[i], rows(ple_w_proj[i], 0))
                down_v = ffn_w_down[i].rearrange("(k q) n -> q k n", q=P)
                with sp.Fori(0, FF2 // 2) as c:
                    load(N_DOWN[i], down_v[:, bass.ds(c * 4, 2), :], c)
                    load(N_DOWN[i] + 1, down_v[:, bass.ds(c * 4 + 2, 2), :], c)
                load(N_DOWN[i] + FF2 - 1, rows(ffn_w_down[i], FT - 2))
                for c in range(4):
                    load(N_GATE[i] + c, cols(ple_w_gate[i], CW * c))
                if i == 1:
                    sp.wait_ge(down_used[i], FF2 - 1)
                    sp.dma_start(gain_final[:, :], norm_final.rearrange("(a n) -> a n", a=1).broadcast_to([P, DM])).then_inc(gain_in, 16)
            for j in range(2 * TB):
                half, t = divmod(j, TB)
                sp.wait_ge(fin_odd if j % 2 else fin_even, j // 2 + 1)
                sp.dma_start(out[0, t * P:(t + 1) * P, half * 512:(half + 1) * 512], result[:, j, :]).then_inc(out_sem, 16)
            sp.wait_ge(out_sem, 16 * 2 * TB)

        @block.gpsimd
        def _(pool):
            count = [0]

            def const(ins):
                count[0] += 1
                ins.then_inc(consts, 1)
                pool.wait_ge(consts, count[0])

            const(pool.memset(gains_nat[:, :], 0.0))
            const(pool.memset(ident[:, :], 0.0))
            const(pool.affine_select(out=ident[:, :], in_=ident[:, :], compare_op=ALU.not_equal, fill=1.0, base=0,
                                     pattern=[[-1, P]], channel_multiplier=1))
            const(pool.memset(minus_half, -0.5))
            const(pool.memset(ones[:, :], 1.0))
            const(pool.memset(neg_ones_f[:, :], -1.0))
            const(pool.affine_select(out=neg_tri_f[:, :], in_=neg_ones_f[:, :], compare_op=ALU.is_ge, fill=0.0, base=0,
                                     pattern=[[-1, P]], channel_multiplier=1))
            const(pool.memset(ident_b[:, :], 0.0))
            const(pool.affine_select(out=ident_b[:, :], in_=ident_b[:, :], compare_op=ALU.not_equal, fill=1.0, base=0,
                                     pattern=[[-1, P]], channel_multiplier=1))
            const(pool.memset(mask_win[:, :, :], 0.0))
            const(pool.affine_select(out=mask_kq[:, :], in_=mask_win[:, 0, :], compare_op=ALU.is_gt, fill=NEG, base=0,
                                     pattern=[[1, P]], channel_multiplier=-1))
            const(pool.affine_select(out=mask_qk[:, :], in_=mask_win[:, 0, :], compare_op=ALU.is_ge, fill=NEG, base=0,
                                     pattern=[[-1, P]], channel_multiplier=1))
            const(pool.memset(gate_zero[:, :], 0.0))
            for half in range(2):
                pool.memset(k_pad[64 * (1 - half):64 * (2 - half), :, half, :], 0.0).then_inc(k_zeroed, 1)
                pool.wait_ge(k_zeroed, half + 1)

            def factor(v):
                pool.wait_ge(mean_done, v + 1)
                pool.tensor_tensor(r_col[:, 4 * v:4 * v + 4], mean_sq, minus_half, ALU.pow).then_inc(r_done, 1)

            def add_squares(v):
                for m in range(1, KT):
                    pool.wait_ge(sq_done, KT * (v - 1) + m + 1)
                    if m > 1:
                        pool.wait_ge(sq_sum_done, (KT - 1) * (v - 1) + m - 1)
                    pool.tensor_tensor(sq_sum[:, :], sq_sum[:, :], sq[:, m % 2, :], ALU.add).then_inc(sq_sum_done, 1)

            def hidden(i, c):
                for j in range(2):
                    pool.wait_ge(silu_done[i], c * 2 + j + 1)
                    pool.wait_ge(u_done[i], c * 2 + j + 1)
                    pool.tensor_tensor(up[:, j, :], gs[:, j, :], up[:, j, :], ALU.mult).then_inc(a_done[i], 1)
                    pool.wait_ge(a_hi_done[i], c * 2 + j + 1)
                    pool.tensor_tensor(act_lo[:, bass.ds((c * 2 + j) * SEQ, SEQ)], up[:, j, :],
                                       act_hi[:, bass.ds((c * 2 + j) * SEQ, SEQ)].bitcast(F32), ALU.subtract).then_inc(a_lo_done[i], 1)

            pool.wait_ge(w_hi_done, 1)
            pool.tensor_tensor(w_lo[:, 0, :], w_raw[:, 0, :], w_hi[:, 0, :].bitcast(F32), ALU.subtract).then_inc(w_lo_done, 1)
            factor(0)
            pool.wait_ge(r_done, 1)
            for j in range(2):
                const(pool.tensor_copy(mask_win[:, 2 * j, :], mask_kq[:, :]))
                const(pool.tensor_copy(mask_win[:, 2 * j + 1, :], mask_qk[:, :]))
            const(pool.tensor_copy(mask_win0[:, 0, :], mask_qk[:, :]))
            const(pool.memset(mask_win0[:, 1, :], NEG))
            const(pool.tensor_copy(mask_win0[:, 2:4, :], mask_win[:, 2:4, :]))
            for j in range(HALF):
                value = float(np.float32(THETA) ** np.float32(-j / HALF))
                const(pool.memset(inv_freq[:, j:j + 1], value))


            for i in L:
                for n in ([n0 + k for n0 in GROUP_CHUNK[1:] for k in (3, 4)] if i == 0 else range(N_IN1 + 2, N_OUT[i] + 2)):
                    pool.wait_ge(w_hi_done, n + 1)
                    pool.wait_ge(w_lo_done, n)
                    pool.tensor_tensor(w_lo[:, n % 2, :], w_raw[:, n % 2, :], w_hi[:, n % 2, :].bitcast(F32), ALU.subtract).then_inc(w_lo_done, 1)
                add_squares(V_MIX[i])
                factor(V_MIX[i])
                with pool.Fori(0, FF2) as c:
                    hidden(i, c)
                add_squares(V_FFN[i])
                factor(V_FFN[i])
                for m in range(KT):
                    if m >= 2:
                        v = V_PLE[i]
                        pool.wait_ge(sq_done, KT * (v - 1) + m)
                        if m > 2:
                            pool.wait_ge(sq_sum_done, (KT - 1) * (v - 1) + m - 2)
                        pool.tensor_tensor(sq_sum[:, :], sq_sum[:, :], sq[:, (m - 1) % 2, :], ALU.add).then_inc(sq_sum_done, 1)
                v = V_PLE[i]
                pool.wait_ge(sq_done, KT * v)
                pool.wait_ge(sq_sum_done, (KT - 1) * (v - 1) + KT - 2)
                pool.tensor_tensor(sq_sum[:, :], sq_sum[:, :], sq[:, (KT - 1) % 2, :], ALU.add).then_inc(sq_sum_done, 1)
                factor(V_PLE[i])

        @block.scalar
        def _(act):
            def split_hi(n, it=0, done=None):
                act.wait_ge(slot_in[n % 2], (n // 2 + it + 1) * 16)
                if n == GATE_CHUNK:
                    act.wait_ge(gate_cols_in, 16)
                if done is None and n >= 2:
                    done = last_product(n - 2)
                if done is not None:
                    act.wait_ge(*done)
                size = KT * P if n == GATE_CHUNK else CHUNK
                act.activation(w_hi[:, n % 2, 0:size], w_raw[:, n % 2, 0:size], ACT.Copy).then_inc(w_hi_done, 1)

            def gained(v, m, hi):
                act.wait_ge(h_done, KT * v + m + 1)
                norm = {0: 0, 1: 2, 2: 4, 3: 1, 4: 3, 5: 5}[v]
                act.activation(hi[:, m, :], h[:, m, :], ACT.Copy, scale=gain_t[:, norm * KT + m:norm * KT + m + 1]).then_inc(x_hi_done, 1)

            def square(v, m):
                act.wait_ge(h_done, KT * v + m + 1)
                if m > 2:
                    act.wait_ge(sq_sum_done, (KT - 1) * (v - 1) + m - 2)
                dst = sq[:, m % 2, :] if m else sq_sum[:, :]
                act.activation(dst, h[:, m, :], ACT.Square).then_inc(sq_done, 1)

            def keep_factor(v):
                act.wait_ge(r_bc_ready, spreads(v))
                act.activation(r_tok[:, :], ps[:, 6, :], ACT.Copy).then_inc(r_bc_done, 1)

            def keep_v(g, t):
                act.wait_ge(v_ready, 4 * g + t + 1)
                act.wait_ge(r_done, 1)
                act.activation(v_nat[:, g % 2, t, :], ps[:, 0 if g else 2 + t % 2, 0:CW], ACT.Copy, scale=r_col[:, t:t + 1]).then_inc(v_done, 1)

            act.preload_act_table_set("natural_log_exp_and_others")
            act.wait_ge(consts, 1)
            for j, gains in enumerate((norm_mix, norm_ffn, norm_ple)):
                act.dma_start(gains_nat[2 * KT * j:2 * KT * (j + 1), :], gains.rearrange("l (k n) -> (l k) n", n=P)).then_inc(gains_in, 16)
            act.dma_start(gate_bias, ev_b_f.rearrange("a f -> f a"), allow_slow_non_contiguous=True).then_inc(small_in[0], 16)
            act.dma_start(sinks, od_sinks.broadcast_to([P, NQ])).then_inc(small_in[1], 16)
            act.dma_start(pos_i[:, :], positions.rearrange("a (t q) -> q (a t)", q=P), allow_slow_non_contiguous=True).then_inc(small_in[2], 16)
            act.wait_ge(gains_t_done, 1)

            def untranspose(m):
                act.wait_ge(xt_ready, m + 1)
                if m > 1:
                    act.wait_ge(h_done, m)
                act.activation(h[:, m, :], ps[:, 2 + m % 6, :], ACT.Copy).then_inc(h_done, 1)

            gained(0, 0, x_hi)
            act.wait_ge(h_done, 1)
            untranspose(1)
            gained(0, 1, x_hi)
            split_hi(0)
            for m in range(2, KT):
                if m % 2:
                    untranspose(m)
                gained(0, m, x_hi)
            split_hi(1)
            for t in range(TB):
                act.wait_ge(x_in[t], 16)
                if t:
                    act.wait_ge(x_sq_done, t)
                act.activation(x_sq[:, :], x_nat[:, t, :], ACT.Square, accum_out=ssq0[:, t:t + 1]).then_inc(x_sq_done, 1)
            keep_factor(0)

            split_hi(2)
            for t in range(TB):
                keep_v(0, t)
            split_hi(3)
            split_hi(4)
            act.wait_ge(consts, 7)
            act.activation(neg_tri[:, :], neg_tri_f[:, :], ACT.Copy)
            act.activation(neg_ones[:, :], neg_ones_f[:, :], ACT.Copy).then_inc(neg_done, 1)

            def front(s):
                buf = B[s % 2]
                if s < 8:
                    act.wait_ge(z_ready, s + 1)
                    act.activation(buf[:, :], z[s % 2], ACT.Abs).then_inc(sb_abs, 1)
                    act.wait_ge(sb_abs, 3 * s + 1)
                    act.activation(buf[:, :], buf[:, :], ACT.Exp, scale=-1.0).then_inc(sb_abs, 1)
                    act.wait_ge(sb_abs, 3 * s + 2)
                    act.activation(buf[:, :], buf[:, :], ACT.Ln, bias=1.0).then_inc(sb_abs, 1)
                else:
                    act.wait_ge(fx_neg, s - 7)
                    for b in range(TB):
                        q = TB - 1 - b
                        part = buf[:, OFF[b]:OFF[b] + LEN[b]]
                        act.activation(part, part, ACT.Exp, bias=neg_max[:, q:q + 1], accum_out=row_sum[:, q:q + 1]).then_inc(fx_exp, 1)

            def keep_l(s):
                act.wait_ge(sb_l, s + 1)
                act.activation(l_hi[:, :], B[2][:, :], ACT.Copy).then_inc(l_hi_done, 1)

            def back(s):
                if s >= 2:
                    act.wait_ge(pv_ready, s - 1)
                if s < 8:
                    act.wait_ge(c_ready, s + 1)
                else:
                    act.wait_ge(fx_t_ready, s - 7)
                act.activation(B[3 + s % 2][:, :], z[s % 2], ACT.Exp if s < 8 else ACT.Copy).then_inc(wt_done, 1)

            def keep_output(s):
                r0, tile = 64 * (s % 2), (4 + s // 2) % 8
                act.wait_ge(pv_ready, s + 1)
                act.activation(o_hi[r0:r0 + 64, tile, :], ps[r0:r0 + 64, 1, :], ACT.Copy).then_inc(o_hi_done, 1)

            front(0)
            act.wait_ge(gate_step, 2)
            act.activation(gate_t[:, :], gate_f[:, :], ACT.Abs).then_inc(gate_abs, 1)
            act.wait_ge(gate_abs, 1)
            act.activation(gate_t[:, :], gate_t[:, :], ACT.Exp, scale=-1.0).then_inc(gate_abs, 1)
            act.wait_ge(gate_abs, 2)
            act.activation(gate_t[:, :], gate_t[:, :], ACT.Ln, bias=1.0).then_inc(gate_abs, 1)
            keep_l(0)
            split_hi(5)
            for s in range(NHEADS):
                g, i = divmod(s, 4)
                early = g < 3 and i < 3
                if early:
                    front(s + 1)
                back(s)
                if not early and s + 1 < NHEADS:
                    front(s + 1)
                if s < 7:
                    keep_l(s + 1)
                if g < 3:
                    if i == 0 and s:
                        act.wait_ge(pv_ready, s)
                    if i < 3:
                        keep_v(g + 1, i)
                    if i == 1:
                        split_hi(GROUP_CHUNK[g + 1] + 2)
                if s:
                    keep_output(s - 1)
                if g < 3 and i == 2:
                    keep_v(g + 1, 3)
                    split_hi(GROUP_CHUNK[g + 1] + 3)
                if g < 3 and i == 3:
                    split_hi(GROUP_CHUNK[g + 1] + 4)
            keep_output(NHEADS - 1)

            for l in L:
                if l == 1:
                    def keep_transposed(u):
                        act.wait_ge(tr_ready, u + 1)
                        t = u % 4
                        if u < 4:
                            act.activation(k1_hi[:, :, t * P:(t + 1) * P], ps[:, turn_bank(u), :].rearrange("q (g n) -> q g n", g=NKV),
                                           ACT.Copy).then_inc(tr_hi_done, 1)
                        else:
                            c = u // 4 - 1
                            for half in range(2):
                                rs = slice(64 * half, 64 * half + 64)
                                ins = act.activation(q1_parts[rs, 2 * c:2 * c + 2, half, t * P:(t + 1) * P],
                                                     ps[rs, turn_bank(u + 4), CW:2 * CW].rearrange("q (g n) -> q g n", g=2), ACT.Copy)
                            ins.then_inc(tr_hi_done, 1)

                    def weights(s):
                        act.wait_ge(s_neg, s + 1)
                        o = 4 * (s % 2)
                        for b in range(TB):
                            act.activation(p1[:, s % 2, b, :], ps[:, 2 + 2 * (s % 2) + b // 2, (b % 2) * 256:(b % 2) * 256 + 256], ACT.Exp,
                                           bias=neg_max[:, o + b:o + b + 1], scale=SCALE,
                                           accum_out=row_sum[:, o + b:o + b + 1]).then_inc(s_exp, 1)
                        act.activation(sink_exp[:, o:o + 4], neg_max[:, o:o + 4], ACT.Exp, bias=sinks[:, s:s + 1]).then_inc(s_exp, 1)

                    split_hi(N_IN1 + 2)
                    for idx in (0, 4, 1, 5, 2, 6, 3, 7, 8, 9, 10, 11):
                        if 4 <= idx < 8:
                            act.wait_ge(in_ready, idx + 1)
                            act.wait_ge(r_done, 4)
                            for d in range(2):
                                ins = act.activation(v1_dup[:, idx - 4, :, d, :], ps[:, bank1(idx), 0:CW].rearrange("q (g n) -> q g n", g=NKV),
                                                     ACT.Copy, scale=r_col[:, 12 + idx - 4:13 + idx - 4])
                            ins.then_inc(v1_done, 1)
                        else:
                            keep_transposed(idx if idx < 4 else idx - 4)
                        if idx in (7, 11):
                            split_hi(N_IN1 + idx // 4 + 2)

                    def keep_output1(s):
                        r0 = 64 * (s % 2)
                        act.wait_ge(pv1_ready, s + 1)
                        act.activation(o_hi[r0:r0 + 64, s // 2, :], ps[r0:r0 + 64, 1, :], ACT.Copy).then_inc(o1_hi_done, 1)

                    keep_transposed(8)
                    weights(0)
                    keep_transposed(9)
                    weights(1)
                    for s in range(NQ):
                        if s == 0:
                            keep_transposed(10)
                        act.wait_ge(t1_ready, s + 1)
                        if s >= 2:
                            act.wait_ge(pv1_ready, s - 1)
                        act.activation(p1_t[:, s % 2, 0:7 * P], ps_flat[:, 6 * 512:6 * 512 + 7 * P], ACT.Copy).then_inc(t1_done, 1)
                        if 0 < s < 10:
                            keep_transposed(10 + s)
                        if s:
                            keep_output1(s - 1)
                        if s + 2 < NQ:
                            weights(s + 2)
                        if s in (1, 5, 9):
                            split_hi(N_IN1 + 5 + s // 4)
                    keep_output1(NQ - 1)
                for m in range(KT):
                    gained(V_MIX[l], m, x_hi)
                    square(V_MIX[l], m)
                    if m % 2:
                        split_hi(N_OUT[l] + m // 2 + 2)
                act.preload_act_table_set("silu_and_others")
                if l == 0:
                    act.wait_ge(trig_step, 1)
                    act.activation(trig[:, :, :, :], ang[:, :, :, :], ACT.Sin).then_inc(trig_done, 1)
                keep_factor(V_MIX[l])

                def hidden(i, c):
                    for j in range(2):
                        act.wait_ge(g_done[i], c * 2 + j + 1)
                        act.activation(gs[:, j, :], gs[:, j, :], ACT.Silu).then_inc(silu_done[i], 1)
                    split_hi(N_FFN[i] + 2, c, (g_ready[i], c * 2 + 2))
                    for j in range(2):
                        act.wait_ge(a_done[i], c * 2 + j + 1)
                        act.activation(act_hi[:, bass.ds((c * 2 + j) * SEQ, SEQ)], up[:, j, :], ACT.Copy).then_inc(a_hi_done[i], 1)
                    split_hi(N_FFN[i] + 3, c, (u_ready[i], c * 2 + 2))

                with act.Fori(0, FF2 - 1) as c:
                    hidden(l, c)
                act.wait_ge(pt_ready[l], 2)
                for j in range(2):
                    act.activation(pt_hi[:, j, :], ps[:, 4 + j, :], ACT.Copy).then_inc(pt_hi_done[l], 1)
                hidden(l, FF2 - 1)
                for m in range(KT):
                    act.wait_ge(e_ready[l], m + 1)
                    act.activation(emb[:, m, :], ps[:, e_bank(m), :], ACT.Copy).then_inc(e_done[l], 1)
                split_hi(N_DOWN[l] + 1)
                with act.Fori(0, FF2 // 2) as c:
                    split_hi(N_DOWN[l] + 2, c, (down_used[l], c * 2 + 1))
                    split_hi(N_DOWN[l] + 3, c, (down_used[l], c * 2 + 2))
                for m in range(KT):
                    gained(V_FFN[l], m, xp_hi)
                    square(V_FFN[l], m)
                split_hi(N_GATE[l] + 1)
                split_hi(N_GATE[l] + 2)
                keep_factor(V_FFN[l])
                for m in range(KT):
                    act.wait_ge(pg_done[l], m + 1)
                    act.activation(ple_t[:, m % 2, :], ple_t[:, m % 2, :], ACT.Sigmoid).then_inc(sig_done[l], 1)
                    if m in (3, 5) and N_GATE[l] + 2 + m // 2 < N_ALL:
                        split_hi(N_GATE[l] + 2 + m // 2)
                    for tile in ([], [0], [1], [2], [3], [4], [5, 6], [7])[m]:
                        if l == 0:
                            gained(3, tile, x_hi)
                        square(V_PLE[l], tile)
                if l == 0:
                    split_hi(N_IN1 + 1)
                    act.preload_act_table_set("natural_log_exp_and_others")
            act.wait_ge(r_done, 7)
            for j in range(0, 2 * TB, 2):
                act.wait_ge(fin_done, j + 1)
                act.activation(result[:, j, :], result[:, j, :], ACT.Copy, scale=r_col[:, 24 + j % TB:25 + j % TB]).then_inc(fin_even, 1)

        @block.vector
        def _(dve):
            def split_lo(n, it=0):
                dve.wait_ge(w_hi_done, n + 1 + 2 * it)
                if n in (1, GROUP_CHUNK[2] + 2, GROUP_CHUNK[3] + 2, N_OUT[0] + 2, N_OUT[1] + 2):
                    dve.wait_ge(w_lo_done, n)
                size = KT * P if n == GATE_CHUNK else CHUNK
                dve.tensor_tensor(w_lo[:, n % 2, 0:size], w_raw[:, n % 2, 0:size], w_hi[:, n % 2, 0:size].bitcast(F32),
                                  ALU.subtract).then_inc(w_lo_done, 1)

            def gained_lo(v, m, hi, lo):
                dve.wait_ge(x_hi_done, KT * v + m + 1)
                norm = {0: 0, 1: 2, 2: 4, 3: 1, 4: 3, 5: 5}[v]
                dve.scalar_tensor_tensor(out=lo[:, m, :], in0=h[:, m, :], scalar=gain_t[:, norm * KT + m:norm * KT + m + 1],
                                         in1=hi[:, m, :].bitcast(F32), op0=ALU.mult, op1=ALU.subtract).then_inc(x_lo_done, 1)

            def mean(v, src):
                dve.tensor_scalar(mean_sq, src, 1.0 / DM, EPS, ALU.mult, ALU.add).then_inc(mean_done, 1)

            def factor(v):
                if v:
                    dve.wait_ge(ssq_ready, v)
                    mean(v, ps[:, 7, 0:TB])
                dve.wait_ge(r_done, v + 1)
                if v == 3:
                    return
                for t in range(TB):
                    ins = dve.tensor_scalar(diag[:, t, :], ident[:, :], r_col[:, 4 * v + t:4 * v + t + 1], None, ALU.mult)
                ins.then_inc(diag_done, 1)

            def add_delta(v, m, bank):
                dve.wait_ge(delta_ready, DELTA[v] + m + 1)
                dve.tensor_tensor(h[:, m, :], ps[:, bank, :], h[:, m, :], ALU.add).then_inc(h_done, 1)

            def keep_qk(g, j):
                slot = (2 * g + j % 2) % 4
                bank0 = 0 if g else j % 2
                dve.wait_ge(qk_ready, 4 * g + j + 1)
                if j < 2:
                    dve.scalar_tensor_tensor(out=q_pair[:, slot, :], in0=ps[:, bank0, :], scalar=SCALE, in1=r_tok[:, :],
                                             op0=ALU.mult, op1=ALU.mult).then_inc(qk_done, 1)
                else:
                    for half in range(2):
                        rs = slice(64 * half, 64 * half + 64)
                        ins = dve.tensor_tensor(k_pad[rs, slot, half, :], ps[rs, bank0, :], r_tok[rs, :], ALU.mult)
                    ins.then_inc(qk_done, 1)

            dve.wait_ge(gains_t_ready, 1)
            dve.tensor_copy(gain_t[:, :], ps[:, 0, 0:P]).then_inc(gains_t_done, 1)
            dve.wait_ge(gains_t_done, 1)
            for m in range(KT):
                if m % 2 == 0:
                    dve.wait_ge(xt_ready, m + 1)
                    if m:
                        dve.wait_ge(h_done, m)
                    dve.tensor_copy(h[:, m, :], ps[:, 2 + m % 6, :]).then_inc(h_done, 1)
                if m:
                    gained_lo(0, m - 1, x_hi, x_lo)
            gained_lo(0, KT - 1, x_hi, x_lo)
            split_lo(1)
            dve.wait_ge(x_sq_done, TB)
            mean(0, ssq0)
            factor(0)

            dve.wait_ge(k_zeroed, 2)
            dve.wait_ge(r_bc_done, 1)
            keep_qk(0, 0)
            keep_qk(0, 1)
            split_lo(2)
            split_lo(3)
            keep_qk(0, 2)
            keep_qk(0, 3)
            split_lo(4)
            dve.wait_ge(gate_ready, 1)
            dve.tensor_tensor(gate_f[:, :], ps[0:NFOX, 7, :], r_tok[0:NFOX, :], ALU.mult).then_inc(gate_step, 1)
            dve.wait_ge(gate_step, 1)
            dve.wait_ge(small_in[0], 16)
            dve.tensor_scalar(gate_f[:, :], gate_f[:, :], gate_bias, None, ALU.add).then_inc(gate_step, 1)

            def front(s):
                zs, buf = z[s % 2], B[s % 2]
                if s < 8:
                    dve.wait_ge(sb_abs, 3 * s + 3)
                    if s:
                        dve.wait_ge(c_ready, s)
                    dve.scalar_tensor_tensor(out=B[2][:, :], in0=zs, scalar=0.0, in1=buf[:, :],
                                             op0=ALU.max, op1=ALU.add).then_inc(sb_l, 1)
                    dve.wait_ge(l_hi_done, s + 1)
                    dve.tensor_tensor(l_lo[:, :], B[2][:, :], l_hi[:, :].bitcast(F32), ALU.subtract).then_inc(l_lo_done, 1)
                else:
                    f = s - 8
                    dve.wait_ge(z_ready, s + 1)
                    dve.wait_ge(f_in, 16 * NFOX)
                    for b in range(TB):
                        q = TB - 1 - b
                        dve.tensor_tensor_reduce(buf[:, OFF[b]:OFF[b] + LEN[b]], zs[:, OFF[b]:OFF[b] + LEN[b]], f_keys[:, f, 0:LEN[b]],
                                                 1.0, LOWEST, ALU.subtract, ALU.max, row_max[:, q:q + 1]).then_inc(fx_max, 1)
                    dve.wait_ge(fx_max, 4 * f + 4)
                    dve.tensor_scalar(neg_max[:, 0:4], row_max[:, 0:4], -1.0, None, ALU.mult).then_inc(fx_neg, 1)
                    dve.wait_ge(fx_exp, 4 * f + 4)
                    dve.reciprocal(row_inv[:, 0:4], row_sum[:, 0:4]).then_inc(fx_inv, 1)
                    dve.wait_ge(fx_inv, f + 1)
                    for b in range(TB):
                        q = TB - 1 - b
                        part = buf[:, OFF[b]:OFF[b] + LEN[b]]
                        ins = dve.tensor_scalar(part, part, row_inv[:, q:q + 1], None, ALU.mult)
                    ins.then_inc(fx_norm, 1)

            def keep_output_lo(s):
                r0, tile = 64 * (s % 2), (4 + s // 2) % 8
                dve.wait_ge(o_hi_done, s + 1)
                dve.tensor_tensor(o_lo[r0:r0 + 64, tile, :], ps[r0:r0 + 64, 1, :], o_hi[r0:r0 + 64, tile, :].bitcast(F32),
                                  ALU.subtract).then_inc(o_lo_done, 1)

            front(0)
            dve.wait_ge(gate_step, 2)
            dve.wait_ge(gate_abs, 3)
            dve.scalar_tensor_tensor(out=gate_f[:, :], in0=gate_f[:, :], scalar=0.0, in1=gate_t[:, :],
                                     op0=ALU.min, op1=ALU.subtract).then_inc(gate_step, 1)
            dve.wait_ge(gate_step, 3)
            dve.wait_ge(consts, 13)
            dve.tensor_tensor_scan(gate_cum[:, :], gate_f[:, :], gate_zero[:, :], 0.0, ALU.add, ALU.add).then_inc(gate_step, 1)
            split_lo(5)
            for s in range(NHEADS):
                g, i = divmod(s, 4)
                early = g < 3 and i < 3
                if early and g >= 2:
                    front(s + 1)
                if g < 3:
                    keep_qk(g + 1, i)
                if early and g < 2:
                    front(s + 1)
                if not early and s + 1 < NHEADS:
                    front(s + 1)
                if g < 3 and i == 1:
                    split_lo(GROUP_CHUNK[g + 1] + 2)
                if s:
                    keep_output_lo(s - 1)
            keep_output_lo(NHEADS - 1)

            for l in L:
                if l == 1:
                    factor(3)
                    for t in range(TB):
                        for table in (cos_t, sin_t):
                            ins = dve.tensor_scalar(table[:, t, :, :], table[:, t, :, :], r_col[:, 12 + t:13 + t], None, ALU.mult)
                    ins.then_inc(table_step, 1)
                    dve.wait_ge(table_step, 2)
                    dve.wait_ge(small_in[1], 16)
                    dve.tensor_scalar(sinks8, sinks, 1.0 / SCALE, None, ALU.mult).then_inc(table_step, 1)
                    dve.wait_ge(table_step, 3)

                    def rotate(idx):
                        u = idx if idx < 4 else idx - 4
                        t = idx % 4
                        dve.wait_ge(in_ready, idx + 1)
                        if u >= 1:
                            dve.wait_ge(tr_ready, u)
                        src = ps[:, bank1(idx), 0:CW].rearrange("q (g e n) -> q g e n", g=4, e=2)
                        a = rope_a[:, :].rearrange("q (g e n) -> q g e n", g=4, e=2)
                        b = rope_b[:, :].rearrange("q (g e n) -> q g e n", g=4, e=2)
                        for e in range(2):
                            dve.tensor_tensor(b[:, :, e, :], src[:, :, 1 - e, :], sin_t[:, t:t + 1, e, :].broadcast_to([P, 4, HALF]), ALU.mult)
                        for e in range(2):
                            ins = dve.tensor_tensor(a[:, :, e, :], src[:, :, e, :], cos_t[:, t:t + 1, e, :].broadcast_to([P, 4, HALF]), ALU.mult)
                        ins.then_inc(rope_step, 1)
                        dve.wait_ge(rope_step, u + 1)
                        if idx < 4:
                            for d in range(2):
                                ins = dve.tensor_tensor(rope_k[:, :, d, :], rope_a[:, :].rearrange("q (g n) -> q g n", g=4),
                                                        rope_b[:, :].rearrange("q (g n) -> q g n", g=4), ALU.add)
                        else:
                            ins = dve.tensor_tensor(rope_q[:, :], rope_a[:, :], rope_b[:, :], ALU.add)
                        ins.then_inc(rope_done, 1)

                    def keep_transposed_lo(idx):
                        u = idx if idx < 4 else idx - 4
                        t = idx % 4
                        dve.wait_ge(tr_hi_done, u + 1)
                        if idx < 4:
                            dve.tensor_tensor(k1_lo[:, :, t * P:(t + 1) * P], ps[:, turn_bank(idx), :].rearrange("q (g n) -> q g n", g=NKV),
                                              k1_hi[:, :, t * P:(t + 1) * P].bitcast(F32), ALU.subtract).then_inc(tr_done, 1)
                            return
                        c = idx // 4 - 2
                        for half in range(2):
                            rs, other = slice(64 * half, 64 * half + 64), slice(64 - 64 * half, 128 - 64 * half)
                            ins = dve.tensor_tensor(q1_parts[other, 2 * c:2 * c + 2, half, t * P:(t + 1) * P],
                                                    ps[rs, turn_bank(idx), CW:2 * CW].rearrange("q (g n) -> q g n", g=2),
                                                    q1_parts[rs, 2 * c:2 * c + 2, half, t * P:(t + 1) * P].bitcast(F32), ALU.subtract)
                        ins.then_inc(tr_done, 1)

                    def maximum(s):
                        o = 4 * (s % 2)
                        dve.wait_ge(s_ready, s + 1)
                        b0 = 2 + 2 * (s % 2)
                        dve.tensor_reduce(row_max[:, o:o + 4], ps[:, b0:b0 + 2, :].rearrange("q b (c n) -> q (b c) n", c=2), AX_X, ALU.max).then_inc(s_max, 1)
                        dve.wait_ge(s_max, s + 1)
                        dve.tensor_scalar(neg_max[:, o:o + 4], row_max[:, o:o + 4], sinks8[:, s:s + 1], -SCALE, ALU.max, ALU.mult).then_inc(s_neg, 1)

                    def normalise(s):
                        o = 4 * (s % 2)
                        dve.wait_ge(s_exp, 5 * s + 5)
                        dve.tensor_tensor(den[:, o:o + 4], row_sum[:, o:o + 4], sink_exp[:, o:o + 4], ALU.add).then_inc(s_den, 1)
                        dve.wait_ge(s_den, s + 1)
                        dve.reciprocal(row_inv[:, o:o + 4], den[:, o:o + 4]).then_inc(s_inv, 1)
                        dve.wait_ge(s_inv, s + 1)
                        for b in range(TB):
                            ins = dve.tensor_scalar(p1[:, s % 2, b, :], p1[:, s % 2, b, :], row_inv[:, o + b:o + b + 1], None, ALU.mult)
                        ins.then_inc(s_norm, 1)

                    for idx in (0, 1, 2, 3, 8, 9, 10, 11, 12):
                        rotate(idx)
                        if idx:
                            keep_transposed_lo(3 if idx == 8 else idx - 1)
                    maximum(0)
                    rotate(13)
                    keep_transposed_lo(12)
                    normalise(0)
                    keep_transposed_lo(13)
                    maximum(1)
                    rotate(14)

                    def keep_output1_lo(s):
                        r0 = 64 * (s % 2)
                        dve.wait_ge(o1_hi_done, s + 1)
                        dve.tensor_tensor(o_lo[r0:r0 + 64, s // 2, :], ps[r0:r0 + 64, 1, :], o_hi[r0:r0 + 64, s // 2, :].bitcast(F32),
                                          ALU.subtract).then_inc(o1_lo_done, 1)

                    for s in range(NQ):
                        if 9 <= s < NQ - 2:
                            maximum(s + 2)
                        if s == 0:
                            keep_transposed_lo(14)
                        if s + 1 < NQ:
                            normalise(s + 1)
                        if 0 < s < 10:
                            keep_transposed_lo(14 + s)
                        if s < 9:
                            maximum(s + 2)
                        if s:
                            keep_output1_lo(s - 1)
                        if s < 9:
                            rotate(15 + s)
                    keep_output1_lo(NQ - 1)
                v = V_MIX[l]
                for m in range(KT):
                    add_delta(v, m, out_bank(m))
                    if m:
                        gained_lo(v, m - 1, x_hi, x_lo)
                    if m == KT - 1:
                        gained_lo(v, m, x_hi, x_lo)
                    if m % 2:
                        split_lo(N_OUT[l] + m // 2 + 2)
                factor(v)
                if l == 0:
                    steps = [0]

                    def step(ins):
                        steps[0] += 1
                        ins.then_inc(rope_angle, 1)
                        dve.wait_ge(rope_angle, steps[0])

                    dve.wait_ge(small_in[2], 16)
                    dve.wait_ge(consts, 52)
                    step(dve.tensor_copy(pos_f, pos_i[:, :]))
                    for e in range(2):
                        for t in range(TB):
                            ins = dve.tensor_scalar(ang[:, e, t, :], inv_freq[:, :], pos_f[:, t:t + 1], None, ALU.mult)
                    step(ins)
                    for e in range(2):
                        ins = dve.tensor_scalar(turns[:, e, :, :], ang[:, e, :, :], 1.0 / (2 * math.pi), 0.25 * e, ALU.mult, ALU.add)
                    step(ins)
                    step(dve.tensor_copy(turns_i[:, :, :, :], turns[:, :, :, :]))
                    step(dve.tensor_copy(turns[:, :, :, :], turns_i[:, :, :, :]))
                    two_pi = 2 * math.pi
                    part1 = 6.28125
                    part2 = math.floor((two_pi - part1) * 2 ** 20) / 2 ** 20
                    part3 = two_pi - part1 - part2
                    for part in (part1, part2, part3):
                        step(dve.scalar_tensor_tensor(out=ang[:, :, :, :].rearrange("q e t n -> q (e t n)"),
                                                      in0=turns[:, :, :, :].rearrange("q e t n -> q (e t n)"), scalar=-part,
                                                      in1=ang[:, :, :, :].rearrange("q e t n -> q (e t n)"), op0=ALU.mult, op1=ALU.add))
                    step(dve.tensor_scalar(ang[:, 1, :, :], ang[:, 1, :, :], math.pi / 2, None, ALU.add))
                    dve.tensor_scalar(ang[:, :, :, :], ang[:, :, :, :], 3.1415925, -3.1415925, ALU.min, ALU.max).then_inc(trig_step, 1)
                    dve.wait_ge(trig_done, 1)
                    for e in range(2):
                        dve.tensor_scalar(cos_t[:, :, e, :], trig[:, 1, :, :], 1.0, None, ALU.mult)
                        ins = dve.tensor_scalar(sin_t[:, :, e, :], trig[:, 0, :, :], 2.0 * e - 1.0, None, ALU.mult)
                    ins.then_inc(table_step, 1)
                dve.wait_ge(r_bc_done, spreads(v))

                def hidden(i, c, first):
                    for j in range(2):
                        dve.wait_ge(g_ready[i], c * 2 + j + 1)
                        if not first:
                            dve.wait_ge(a_done[i], c * 2 + j - 1)
                        dve.tensor_tensor(gs[:, j, :], ps[:, j, :], r_tok[:, :], ALU.mult).then_inc(g_done[i], 1)
                    split_lo(N_FFN[i] + 2, c)
                    for j in range(2):
                        dve.wait_ge(u_ready[i], c * 2 + j + 1)
                        if not first:
                            dve.wait_ge(a_lo_done[i], c * 2 + j - 1)
                        dve.tensor_tensor(up[:, j, :], ps[:, 2 + j, :], r_tok[:, :], ALU.mult).then_inc(u_done[i], 1)
                    split_lo(N_FFN[i] + 3, c)

                hidden(l, 0, True)
                with dve.Fori(1, FF2 - 1) as c:
                    hidden(l, c, False)
                for j in range(2):
                    dve.wait_ge(pt_hi_done[l], j + 1)
                    dve.tensor_tensor(pt_lo[:, j, :], ps[:, 4 + j, :], pt_hi[:, j, :].bitcast(F32), ALU.subtract).then_inc(pt_lo_done[l], 1)
                hidden(l, FF2 - 1, False)
                split_lo(N_DOWN[l] + 1)
                with dve.Fori(0, FF2 // 2) as c:
                    split_lo(N_DOWN[l] + 2, c)
                    split_lo(N_DOWN[l] + 3, c)
                v = V_FFN[l]
                for m in range(KT):
                    add_delta(v, m, m)
                    if m:
                        gained_lo(v, m - 1, xp_hi, xp_lo)
                gained_lo(v, KT - 1, xp_hi, xp_lo)
                split_lo(N_GATE[l] + 1)
                factor(v)
                split_lo(N_GATE[l] + 2)
                dve.wait_ge(r_bc_done, spreads(v))
                v = V_PLE[l]

                def add_embedding(m):
                    dve.wait_ge(sig_done[l], m + 1)
                    dve.tensor_tensor(ple_t[:, m % 2, :], ple_t[:, m % 2, :], emb[:, m, :], ALU.mult).then_inc(d_done[l], 1)
                    dve.wait_ge(d_done[l], m + 1)
                    dve.tensor_tensor(h[:, m, :], h[:, m, :], ple_t[:, m % 2, :], ALU.add).then_inc(h_done, 1)

                for m in range(KT):
                    dve.wait_ge(pg_ready[l], m + 1)
                    if m >= 2:
                        dve.wait_ge(h_done, KT * v + m - 1)
                    dve.tensor_tensor(ple_t[:, m % 2, :], ps[:, m % 4, :], r_tok[:, :], ALU.mult).then_inc(pg_done[l], 1)
                    if 0 < m < KT - 1:
                        add_embedding(m - 1)
                    if m >= KT - 2:
                        add_embedding(m)
                    if m in (3, 5) and N_GATE[l] + 2 + m // 2 < N_ALL:
                        split_lo(N_GATE[l] + 2 + m // 2)
                    if l == 0:
                        for tile in ([], [], [0], [1], [2], [3], [4, 5, 6], [7])[m]:
                            gained_lo(3, tile, x_hi, x_lo)
                if l == 0:
                    split_lo(N_IN1 + 1)

            dve.wait_ge(gain_in, 16)
            for j in range(2 * TB):
                half, t = divmod(j, TB)
                dve.wait_ge(fin_ready, j + 1)
                dve.tensor_tensor(result[:, j, :], ps[:, fin_bank(j), :], gain_final[:, half * 512:(half + 1) * 512], ALU.mult).then_inc(fin_done, 1)
                if j == 4:
                    dve.wait_ge(ssq_ready, 6)
                    mean(6, ps[:, 7, 0:TB])
            dve.wait_ge(r_done, 7)
            dve.wait_ge(fin_done, 2 * TB)
            for j in range(1, 2 * TB, 2):
                dve.tensor_scalar(result[:, j, :], result[:, j, :], r_col[:, 24 + j % TB:25 + j % TB], None, ALU.mult).then_inc(fin_odd, 1)

        @block.tensor
        def _(pe):
            def weights(n, it=0):
                pe.wait_ge(w_lo_done, n + 1 + 2 * it)

            def split_product(outp, slot, cols_of, hi, lo, kts, ready=None, first=True, last=True):
                for a, kt in enumerate(kts):
                    if ready is not None:
                        pe.wait_ge(*ready(kt))
                    c0 = cols_of(kt)
                    wh, wl = w_hi[:, slot, c0:c0 + P], w_lo[:, slot, c0:c0 + P]
                    pe.matmul(outp, wh, hi(kt), start=first and a == 0, stop=False)
                    pe.matmul(outp, wl, hi(kt), start=False, stop=False)
                    ins = pe.matmul(outp, wh, lo(kt), start=False, stop=last and a == len(kts) - 1)
                return ins

            def split_product_nat(outp, slot, t, ready=None, kts=range(KT)):
                for kt in kts:
                    if ready is not None:
                        pe.wait_ge(*ready(kt))
                    c0 = kt * CW
                    wh, wl = w_hi[:, slot, c0:c0 + CW], w_lo[:, slot, c0:c0 + CW]
                    xh, xl = x_hi[:, kt, t * P:(t + 1) * P], x_lo[:, kt, t * P:(t + 1) * P]
                    pe.matmul(outp, xh, wh, start=kt == 0, stop=False)
                    pe.matmul(outp, xh, wl, start=False, stop=False)
                    ins = pe.matmul(outp, xl, wh, start=False, stop=kt == KT - 1)
                return ins

            def xh(kt):
                return x_hi[:, kt, :]

            def xl(kt):
                return x_lo[:, kt, :]

            def square_sums(v):
                pe.wait_ge(sq_sum_done, (KT - 1) * v)
                for t in range(TB):
                    ins = pe.matmul(ps[:, 7, t:t + 1], sq_sum[:, t * P:(t + 1) * P], ones[:, 0:1], start=True, stop=True)
                ins.then_inc(ssq_ready, 1)

            def spread_factor(v):
                pe.wait_ge(diag_done, spreads(v))
                pe.matmul(ps[:, 6, :], ones[:, :], diag[:, :, :].rearrange("q t n -> q (t n)"), start=True, stop=True).then_inc(r_bc_ready, 1)

            pe.wait_ge(consts, 3)
            pe.wait_ge(gains_in, 48)
            pe.transpose(ps[:, 0, 0:P], gains_nat[:, :], ident[:, :]).then_inc(gains_t_ready, 1)
            for t in range(TB):
                pe.wait_ge(x_in[t], 16)
            for kt in range(KT):
                if kt >= 6:
                    pe.wait_ge(h_done, kt - 5)
                for t in range(TB):
                    ins = pe.transpose(ps[:, 2 + kt % 6, t * P:(t + 1) * P], x_nat[:, t, kt * P:(kt + 1) * P], ident[:, :])
                ins.then_inc(xt_ready, 1)

            def project_out(l, m, steps):
                n = N_OUT[l] + m // 2
                weights(n)
                if m >= 3:
                    pe.wait_ge(h_done, KT * V_MIX[l] + m - 1)
                o_ready = o1_lo_done if l else o_lo_done
                for a in steps:
                    kt = a if l else (a + 4) % KT
                    if m < 2:
                        pe.wait_ge(o_ready, 2 * a + 2)
                    ins = split_product(ps[:, out_bank(m), :], n % 2, lambda kt: kt * CW + (m % 2) * P, lambda kt: o_hi[:, kt, :],
                                        lambda kt: o_lo[:, kt, :], [kt], first=a == 0, last=a == KT - 1)
                if steps[-1] == KT - 1:
                    ins.then_inc(delta_ready, 1)

            def project_qk(g, j):
                n = GROUP_CHUNK[g] + (0 if j < 2 else 2)
                weights(n)
                if g == 0 and j >= 2:
                    pe.wait_ge(qk_done, j - 1)
                if g:
                    pe.wait_ge(qk_done, 4 * g + j)
                    pe.wait_ge(v_done, 4 * g + (4 if j == 3 else j))
                ready = (lambda kt: (x_lo_done, kt + 1)) if 4 * g + j == 0 else None
                split_product(ps[:, 0 if g else j % 2, :], n % 2, lambda kt: kt * CW + (j % 2) * P, xh, xl, range(KT), ready).then_inc(qk_ready, 1)

            def project_v(g, t):
                n = GROUP_CHUNK[g] + 1
                weights(n)
                if g == 0 and t >= 2:
                    pe.wait_ge(v_done, t - 1)
                if g:
                    pe.wait_ge(v_done, 4 * g + t)
                    pe.wait_ge(qk_done, 4 * g + min(t, 2) + 1)
                split_product_nat(ps[:, 0 if g else 2 + t % 2, 0:CW], n % 2, t).then_inc(v_ready, 1)

            project_qk(0, 0)
            project_qk(0, 1)
            project_v(0, 0)
            spread_factor(0)
            for t in range(1, TB):
                project_v(0, t)
            project_qk(0, 2)
            project_qk(0, 3)
            weights(GATE_CHUNK)
            split_product(ps[:, 7, :], GATE_CHUNK % 2, lambda kt: kt * P, xh, xl, range(KT)).then_inc(gate_ready, 1)

            def part(region, b, c0, width):
                return region[:, OFF[b] + c0:OFF[b] + c0 + width]

            def scores0(s):
                g, i = divmod(s, 4)
                slot, half = (2 * g + i // 2) % 4, i % 2
                pe.wait_ge(qk_done, 4 * g + 4)
                if s == 1:
                    pe.wait_ge(gate_step, 1)
                if s >= 2:
                    pe.wait_ge(wt_done, s - 1)
                for b in (0, 1, 3, 2):
                    q = TB - 1 - b
                    keys = k_pad[:, slot, half, b * P:(b + 1) * P] if g < 2 else k_pad[:, slot, half, 0:LEN[b]]
                    queries = q_pair[:, slot, b * P:SEQ] if g < 2 else q_pair[:, slot, q * P:(q + 1) * P]
                    lhs, rhs = (keys, queries) if g < 2 else (queries, keys)
                    pe.matmul(part(z[s % 2], b, 0, LEN[b]), lhs, rhs, start=b != 3, stop=False, skip_group_check=True)
                    ins = pe.matmul(part(z[s % 2], b, 0 if g < 2 else q * P, P), ident_b[:, :], (mask_kq if g < 2 else mask_qk)[:, :],
                                    start=False, stop=g >= 2, skip_group_check=True)
                ins.then_inc(z_ready, 1)

            def sums0(s):
                pe.wait_ge(neg_done, 1)
                pe.wait_ge(l_lo_done, s + 1)
                for b in range(TB):
                    for j in range(b, TB):
                        dst, neg = part(z[s % 2], b, (j - b) * P, LEN[j]), (neg_tri if j == b else neg_ones)[:, :]
                        if LEN[j] > P:
                            pe.matmul(dst, neg, part(l_hi, j, 0, LEN[j]), start=False, stop=False, skip_group_check=True)
                            pe.matmul(dst, neg, part(l_lo, j, 0, LEN[j]), start=False, stop=False, skip_group_check=True)
                        else:
                            ins = pe.matmul(dst, neg.bitcast(F32), part(B[2], j, 0, LEN[j]), start=False, stop=True, skip_group_check=True)
                ins.then_inc(c_ready, 1)

            def turn0(s):
                pe.wait_ge(fx_norm, s - 7)
                for b in range(TB):
                    for q in range(b, TB):
                        ins = pe.transpose(part(z[s % 2], b, (q - b) * P, P), part(B[s % 2], TB - 1 - q, b * P, P), ident[:, :])
                ins.then_inc(fx_t_ready, 1)

            def output0(s):
                g, i = divmod(s, 4)
                pe.wait_ge(wt_done, s + 1)
                pe.wait_ge(v_done, 4 * g + 4)
                if s:
                    pe.wait_ge(o_lo_done, s)
                for b in range(TB):
                    ins = pe.matmul(ps[:, 1, b * P:SEQ], v_nat[:, g % 2, b, (i // 2) * P:(i // 2 + 1) * P], part(B[3 + s % 2], b, 0, LEN[b]),
                                    start=b == 0, stop=b == TB - 1, skip_group_check=True)
                ins.then_inc(pv_ready, 1)

            pe.wait_ge(consts, 12)
            pe.wait_ge(v_done, 4)
            scores0(0)
            for s in range(NHEADS):
                g, i = divmod(s, 4)
                middle = sums0 if g < 2 else turn0
                if g == 3 or i < 3:
                    if s + 1 < NHEADS:
                        scores0(s + 1)
                    else:
                        project_out(0, 0, range(KT - 1))
                    if g < 3:
                        project_qk(g + 1, i)
                    middle(s)
                else:
                    project_qk(g + 1, i)
                    middle(s)
                    scores0(s + 1)
                if g < 3 and i < 3:
                    project_v(g + 1, i)
                if s:
                    output0(s - 1)
                if g < 3 and i == 2:
                    project_v(g + 1, 3)
            project_out(0, 1, range(KT - 1))
            output0(NHEADS - 1)

            for l in L:
                if l == 1:
                    pe.wait_ge(consts, 20)

                    def project(idx, kts=range(KT)):
                        c, t = divmod(idx, 4)
                        weights(N_IN1 + c)
                        if idx < 4:
                            pe.wait_ge(pg_done[0], idx + 5)
                        elif idx >= 6:
                            prev = idx - 6 if idx < 8 else idx - 2 if idx < 15 else idx - 1
                            if 4 <= prev < 8:
                                pe.wait_ge(v1_done, prev - 3)
                            else:
                                pe.wait_ge(rope_step, (prev if prev < 4 else prev - 4) + 1)
                            if prev >= 14:
                                pe.wait_ge(tr_done, prev - 3)
                        ready = (lambda kt: (x_lo_done, 3 * KT + kt + 1)) if idx == 0 else None
                        ins = split_product_nat(ps[:, bank1(idx), 0:CW], (N_IN1 + c) % 2, t, ready, kts)
                        if kts[-1] == KT - 1:
                            ins.then_inc(in_ready, 1)

                    def turn(idx):
                        if idx < 4:
                            pe.wait_ge(rope_done, idx + 1)
                            if idx >= 2:
                                pe.wait_ge(tr_done, idx - 1)
                            for g in range(NKV):
                                ins = pe.transpose(ps[:, turn_bank(idx), g * P:(g + 1) * P], rope_k[:, g, :, :].rearrange("q d n -> q (d n)"), ident[:, :])
                        else:
                            pe.wait_ge(rope_done, idx - 3)
                            if idx < 14:
                                pe.wait_ge(tr_done, idx - 5)
                            for j in range(2):
                                ins = pe.transpose(ps[:, turn_bank(idx), CW + j * P:CW + (j + 1) * P], rope_q[:, j * P:(j + 1) * P], ident[:, :])
                        ins.then_inc(tr_ready, 1)

                    def scores(s):
                        g, half, b0 = s // 4, s % 2, 2 + 2 * (s % 2)
                        pe.wait_ge(tr_done, 4 + 4 * g + 4)
                        if s >= 2:
                            pe.wait_ge(s_exp, 5 * (s - 1))
                        for b in range(TB):
                            dst = ps[:, b0 + b // 2, :]
                            if b % 2 == 0:
                                mask = mask_win0 if b == 0 else mask_win
                                pe.matmul(dst, ident_b[:, :], mask[:, :, :].rearrange("q a n -> q (a n)"), start=True, stop=False, skip_group_check=True)
                            k0 = max(b - 1, 0)
                            for keys in (k1_hi, k1_lo):
                                ins = pe.matmul(dst[:, (b % 2) * 256:(b % 2) * 256 + 256], q1_parts[:, s // 2, half, b * P:(b + 1) * P],
                                                keys[:, g, k0 * P:(k0 + 2) * P], start=False, stop=keys is k1_lo, skip_group_check=True)
                        ins.then_inc(s_ready, 1)

                    for idx in range(4):
                        if idx == 3:
                            square_sums(3)
                        project(idx, range(KT - 1))
                    for idx in range(13):
                        project(idx, [KT - 1] if idx < 4 else range(KT))
                        if 4 <= idx < 8:
                            turn(idx - 4)
                        if idx >= 9:
                            turn(idx - 1)

                    def turn_weights(s):
                        pe.wait_ge(s_norm, s + 1)
                        if s:
                            pe.wait_ge(t1_done, s)
                        else:
                            pe.wait_ge(tr_done, 10)
                        for b in range(TB):
                            for j in range(min(2, TB - b)):
                                c0 = (2 * b + j) * P
                                p0 = P if j == 0 and b else 0
                                ins = pe.transpose(ps_flat[:, 6 * 512 + c0:6 * 512 + c0 + P], p1[:, s % 2, b + j, p0:p0 + P], ident[:, :])
                        ins.then_inc(t1_ready, 1)

                    def output(s):
                        pe.wait_ge(t1_done, s + 1)
                        pe.wait_ge(v1_done, 4)
                        if s:
                            pe.wait_ge(o1_lo_done, s)
                        for b in range(TB):
                            width = min(2, TB - b) * P
                            ins = pe.matmul(ps[:, 1, b * P:b * P + width], v1_dup[:, b, s // 4, :, :].rearrange("q d n -> q (d n)"),
                                            p1_t[:, s % 2, 2 * b * P:2 * b * P + width], start=b == 0, stop=b == TB - 1, skip_group_check=True)
                        ins.then_inc(pv1_ready, 1)

                    project(13)
                    scores(0)
                    turn(12)
                    project(14)
                    scores(1)
                    turn(13)
                    for s in range(NQ):
                        if s == NQ - 1:
                            project_out(1, 0, range(KT - 1))
                        if 9 <= s < NQ - 2:
                            scores(s + 2)
                        turn_weights(s)
                        if s == NQ - 1:
                            project_out(1, 1, range(KT - 1))
                        if s < 9:
                            scores(s + 2)
                        if s < 10:
                            turn(14 + s)
                        if s:
                            output(s - 1)
                        if s < 9:
                            project(15 + s)
                    output(NQ - 1)

                v = V_MIX[l]
                for m in range(KT):
                    if m < 2:
                        project_out(l, m, [KT - 1])
                    else:
                        project_out(l, m, range(KT))

                def hidden(c, first):
                    for j in range(2):
                        weights(N_FFN[l], c)
                        if not first:
                            pe.wait_ge(g_done[l], c * 2 + j - 1)
                        ready = (lambda kt: (x_lo_done, KT * v + kt + 1)) if first and j == 0 else None
                        split_product(ps[:, j, :], N_FFN[l] % 2, lambda kt: kt * CW + j * P, xh, xl, range(KT), ready).then_inc(g_ready[l], 1)
                        if first and j == 0:
                            square_sums(v)
                        if first and j == 1:
                            spread_factor(v)
                    for j in range(2):
                        weights(N_FFN[l] + 1, c)
                        if not first:
                            pe.wait_ge(u_done[l], c * 2 + j - 1)
                        split_product(ps[:, 2 + j, :], (N_FFN[l] + 1) % 2, lambda kt: kt * CW + j * P, xh, xl, range(KT)).then_inc(u_ready[l], 1)

                hidden(0, True)
                with pe.Fori(1, FF2 - 1) as c:
                    hidden(c, False)
                pe.wait_ge(p_in[l], 16)
                for j in range(2):
                    for t in range(TB):
                        ins = pe.transpose(ps[:, 4 + j, t * P:(t + 1) * P], p_nat[:, t, j * P:(j + 1) * P], ident[:, :])
                    ins.then_inc(pt_ready[l], 1)
                hidden(FF2 - 1, False)

                n = N_EMB[l]
                weights(n)
                for m in range(KT):
                    if m >= 4:
                        pe.wait_ge(e_done[l], m - 3)
                    ready = (lambda kt: (pt_lo_done[l], kt + 1)) if m == 0 else None
                    split_product(ps[:, e_bank(m), :], n % 2, lambda kt: kt * DM + m * P, lambda kt: pt_hi[:, kt, :],
                                  lambda kt: pt_lo[:, kt, :], range(2), ready).then_inc(e_ready[l], 1)

                def down(n, it, first):
                    weights(n, it)
                    d = n - N_DOWN[l]
                    pe.wait_ge(a_lo_done[l], 2 * d + 2 + it * 4)
                    if first:
                        pe.wait_ge(u_done[l], FT)
                    for m in range(KT):
                        if first and m == 4:
                            pe.wait_ge(e_done[l], KT)
                        for j in range(2):
                            k0 = (2 * d + j) * SEQ + it * (4 * SEQ)
                            wh = w_hi[:, n % 2, j * DM + m * P:j * DM + (m + 1) * P]
                            wl = w_lo[:, n % 2, j * DM + m * P:j * DM + (m + 1) * P]
                            ah = act_hi[:, bass.ds(k0, SEQ)]
                            al = act_lo[:, bass.ds(k0, SEQ)]
                            last = d == FF2 - 1 and j == 1
                            pe.matmul(ps[:, m, :], wh, ah, start=first and j == 0, stop=False, skip_group_check=True)
                            pe.matmul(ps[:, m, :], wl, ah, start=False, stop=False, skip_group_check=True)
                            ins = pe.matmul(ps[:, m, :], wh, al, start=False, stop=last, skip_group_check=True)
                        if d == FF2 - 1:
                            ins.then_inc(delta_ready, 1)
                    if d < FF2 - 1:
                        ins.then_inc(down_used[l], 1)

                down(N_DOWN[l], 0, True)
                down(N_DOWN[l] + 1, 0, False)
                with pe.Fori(1, FF2 // 2) as c:
                    down(N_DOWN[l], c, False)
                    down(N_DOWN[l] + 1, c, False)
                down(N_DOWN[l] + FF2 - 1, 0, False)

                v = V_FFN[l]
                for m in range(KT):
                    n = N_GATE[l] + m // 2
                    weights(n)
                    if m >= 4:
                        pe.wait_ge(pg_done[l], m - 3)
                    ready = (lambda kt: (x_lo_done, KT * v + kt + 1)) if m == 0 else None
                    split_product(ps[:, m % 4, :], n % 2, lambda kt: kt * CW + (m % 2) * P, lambda kt: xp_hi[:, kt, :],
                                  lambda kt: xp_lo[:, kt, :], range(KT), ready).then_inc(pg_ready[l], 1)
                    if m == 1:
                        square_sums(v)
                    if m == 2:
                        spread_factor(v)

            for half in range(2):
                for kt in range(4 * half, 4 * half + 4):
                    pe.wait_ge(h_done, KT * 6 + kt + 1)
                for t in range(TB):
                    j = half * TB + t
                    if 3 <= j < 7:
                        pe.wait_ge(pg_done[1], j + 2)
                    if j == 7:
                        pe.wait_ge(fin_done, 1)
                    for a in range(4):
                        ins = pe.transpose(ps[:, fin_bank(j), a * P:(a + 1) * P], h[:, 4 * half + a, t * P:(t + 1) * P], ident[:, :])
                    ins.then_inc(fin_ready, 1)
            square_sums(6)


_INS = ["x", "p", "positions", "norm_mix", "norm_ffn", "norm_ple", "norm_final", "ev_w_in", "ev_b_f", "ev_w_out",
        "od_w_in", "od_sinks", "od_w_out", "ffn_w_gate", "ffn_w_up", "ffn_w_down", "ple_w_proj", "ple_w_gate"]


def kernel(**inputs):
    import numpy as _np
    import concourse.bacc as _bacc
    from concourse import mybir as _mybir
    from concourse.bass_utils import run_bass_kernel_spmd as _run

    nc = _bacc.Bacc("TRN2", target_bir_lowering=False, num_devices=1, dynamic_dma_scratch_size=4096)
    arrays, args = {}, []
    for name in _INS:
        a = _np.ascontiguousarray(inputs[name])
        arrays[f"in_{name}"] = a
        args.append(nc.dram_tensor(f"in_{name}", a.shape, _mybir.dt.from_np(a.dtype), kind="ExternalInput").ap())
    shape = arrays["in_x"].shape
    args.append(nc.dram_tensor("out_0", shape, _mybir.dt.from_np(_np.dtype("float32")), kind="ExternalOutput").ap())
    hybrid_trunk(nc, *args)
    r = _run(nc, [arrays], core_ids=[0])
    return r.results[0]["out_0"]
```
